# Optimizing a Trainium2 kernel written in Bass

```python
import math
import jax, jax.numpy as jnp
from jax import lax
import numpy as np

D_MODEL = 1024
BATCH = 1
SEQ = 512
DEPTH = 1
DEC_BATCH = 1
DEC_SEQ = 32
PAST_LEN = 1024

CHUNK = 64
N_META = 16
CONV_CH = 512
CONV_WIDTH = 31
SB_HEADS = 8
SB_HEAD_DIM = 64
SB_WIDTH = SB_HEADS * SB_HEAD_DIM
MIX_WIDTH = CONV_CH + SB_WIDTH
IN_WIDTH = 2 * CONV_CH + 3 * SB_WIDTH
Q_BLOCK = 128
N_GROUPS = 4
EXPERTS_PER_GROUP = 8
N_EXPERTS = N_GROUPS * EXPERTS_PER_GROUP
TOP_K = 2
D_EXPERT = 256
EPS = 1e-6

kernel_name = 'hymba_conformer_stickbreak_hmoe_stream'

def rmsnorm(x, g):
    xf = x.astype(jnp.float32)
    y = xf * lax.rsqrt(jnp.mean(xf * xf, axis=-1, keepdims=True) + EPS)
    return (y * g.astype(jnp.float32)).astype(x.dtype)

def layernorm(x, g, b):
    xf = x.astype(jnp.float32)
    mu = jnp.mean(xf, axis=-1, keepdims=True)
    var = jnp.mean(jnp.square(xf - mu), axis=-1, keepdims=True)
    y = (xf - mu) * lax.rsqrt(var + EPS)
    return (y * g.astype(jnp.float32) + b.astype(jnp.float32)).astype(x.dtype)

def causal_dwconv(u_hist, w, b):
    y = lax.conv_general_dilated(u_hist, w[:, None, :], window_strides=(1,), padding='VALID',
                                 dimension_numbers=('NWC', 'WIO', 'NWC'),
                                 feature_group_count=CONV_CH)
    return y + b

def sb_block(q, k, v, q_start):
    scale = 1.0 / math.sqrt(SB_HEAD_DIM)
    z = jnp.einsum('bqhd,bkhd->bhqk', q.astype(jnp.float32), k.astype(jnp.float32)) * scale
    t = q_start + jnp.arange(q.shape[1])
    s = jnp.arange(k.shape[1])
    vis = s[None, :] < t[:, None]
    log_keep = jnp.where(vis, jax.nn.log_sigmoid(-z), 0.0)
    later = lax.cumsum(log_keep, axis=3, reverse=True) - log_keep
    w = jnp.where(vis, jnp.exp(jax.nn.log_sigmoid(z) + later), 0.0)
    return jnp.einsum('bhqk,bkhd->bqhd', w, v.astype(jnp.float32))

def stick_breaking(q, k, v, q_start):
    tq = q.shape[1]
    outs = []
    for s0 in range(0, tq, Q_BLOCK):
        s1 = min(s0 + Q_BLOCK, tq)
        n_keys = q_start + s1
        outs.append(sb_block(q[:, s0:s1], k[:, :n_keys], v[:, :n_keys], q_start + s0))
    return jnp.concatenate(outs, axis=1)

def head_rmsnorm(o, g):
    y = o * lax.rsqrt(jnp.mean(o * o, axis=-1, keepdims=True) + EPS)
    b, t = o.shape[0], o.shape[1]
    return y.reshape(b, t, SB_WIDTH) * g.astype(jnp.float32)

def hier_moe(h, w_rg, b_rg, w_re, b_re, w_e_in, w_e_out):
    b, t, d = h.shape
    hf = h.reshape(b * t, d)
    lg = (hf @ w_rg).astype(jnp.float32) + b_rg.astype(jnp.float32)
    p_g = jax.nn.softmax(lg, axis=-1)
    g_sel = jnp.argmax(lg, axis=-1)
    p_g_sel = jnp.max(p_g, axis=-1, keepdims=True)
    le = ((hf @ w_re).astype(jnp.float32) + b_re.astype(jnp.float32)).reshape(-1, N_GROUPS, EXPERTS_PER_GROUP)
    le_sel = jnp.einsum('nge,ng->ne', le, jax.nn.one_hot(g_sel, N_GROUPS, dtype=jnp.float32))
    p_e = jax.nn.softmax(le_sel, axis=-1)
    top_p, top_i = lax.top_k(p_e, TOP_K)
    top_p = top_p / jnp.sum(top_p, axis=-1, keepdims=True)
    expert_id = g_sel[:, None] * EXPERTS_PER_GROUP + top_i
    gates = jnp.sum(jax.nn.one_hot(expert_id, N_EXPERTS, dtype=jnp.float32)
                    * (p_g_sel * top_p)[..., None], axis=1)
    out = jnp.zeros((b * t, d), jnp.float32)
    for e in range(N_EXPERTS):
        gu = hf @ w_e_in[e]
        act = jax.nn.silu(gu[:, :D_EXPERT]) * gu[:, D_EXPERT:]
        out = out + gates[:, e:e + 1] * (act @ w_e_out[e]).astype(jnp.float32)
    return out.astype(h.dtype).reshape(b, t, d)

def layer(x, conv_hist, k_past, v_past, p):
    (g_mix, w_in, conv_w, conv_b, ln_g, ln_b, g_sb, w_out,
     g_ffn, w_rg, b_rg, w_re, b_re, w_e_in, w_e_out) = p
    b, t, _ = x.shape
    h = rmsnorm(x, g_mix)
    proj = h @ w_in
    a_val, a_gate, q, k, v = jnp.split(
        proj, [CONV_CH, 2 * CONV_CH, 2 * CONV_CH + SB_WIDTH, 2 * CONV_CH + 2 * SB_WIDTH], axis=-1)
    u = a_val * jax.nn.sigmoid(a_gate)
    u_hist = jnp.concatenate([conv_hist, u], axis=1)
    a_out = jax.nn.silu(layernorm(causal_dwconv(u_hist, conv_w, conv_b), ln_g, ln_b))
    q = q.reshape(b, t, SB_HEADS, SB_HEAD_DIM)
    k = k.reshape(b, t, SB_HEADS, SB_HEAD_DIM)
    v = v.reshape(b, t, SB_HEADS, SB_HEAD_DIM)
    if k_past is None:
        k_all, v_all, q_start = k, v, 0
    else:
        k_all = jnp.concatenate([k_past, k], axis=1)
        v_all = jnp.concatenate([v_past, v], axis=1)
        q_start = k_past.shape[1]
    b_out = head_rmsnorm(stick_breaking(q, k_all, v_all, q_start), g_sb).astype(x.dtype)
    x = x + jnp.concatenate([a_out, b_out], axis=-1) @ w_out
    x = x + hier_moe(rmsnorm(x, g_ffn), w_rg, b_rg, w_re, b_re, w_e_in, w_e_out)
    return x, k, v, u_hist[:, -(CONV_WIDTH - 1):]

def setup_inputs(seed: int = 0) -> dict:
    key = jax.random.key(seed)
    ks = jax.random.split(key, 24)
    f32 = jnp.float32
    nrm = lambda k, shape, s: jax.random.normal(k, shape, f32) * s
    return {
        'x_prompt': nrm(ks[0], (BATCH, SEQ, D_MODEL), 1.0),
        'x_sample': nrm(ks[1], (DEC_BATCH, DEC_SEQ, D_MODEL), 1.0),
        'cache_k': nrm(ks[2], (DEPTH, DEC_BATCH, PAST_LEN, SB_HEADS, SB_HEAD_DIM), 1.0),
        'cache_v': nrm(ks[3], (DEPTH, DEC_BATCH, PAST_LEN, SB_HEADS, SB_HEAD_DIM), 1.0),
        'cache_conv': nrm(ks[4], (DEPTH, DEC_BATCH, CONV_WIDTH - 1, CONV_CH), 0.5),
        'meta_tokens': nrm(ks[5], (N_META, D_MODEL), 1.0),
        'g_mix': 1.0 + nrm(ks[6], (DEPTH, D_MODEL), 0.02),
        'w_in': nrm(ks[7], (DEPTH, D_MODEL, IN_WIDTH), D_MODEL ** -0.5),
        'conv_w': nrm(ks[8], (DEPTH, CONV_WIDTH, CONV_CH), CONV_WIDTH ** -0.5),
        'conv_b': nrm(ks[9], (DEPTH, CONV_CH), 0.02),
        'conv_ln_g': 1.0 + nrm(ks[10], (DEPTH, CONV_CH), 0.02),
        'conv_ln_b': nrm(ks[11], (DEPTH, CONV_CH), 0.02),
        'g_sb': 1.0 + nrm(ks[12], (DEPTH, SB_WIDTH), 0.02),
        'w_out': nrm(ks[13], (DEPTH, MIX_WIDTH, D_MODEL), MIX_WIDTH ** -0.5),
        'g_ffn': 1.0 + nrm(ks[14], (DEPTH, D_MODEL), 0.02),
        'w_router_group': nrm(ks[15], (DEPTH, D_MODEL, N_GROUPS), D_MODEL ** -0.5),
        'b_router_group': nrm(ks[16], (DEPTH, N_GROUPS), 0.01),
        'w_router_expert': nrm(ks[17], (DEPTH, D_MODEL, N_EXPERTS), D_MODEL ** -0.5),
        'b_router_expert': nrm(ks[18], (DEPTH, N_EXPERTS), 0.01),
        'w_expert_in': nrm(ks[19], (DEPTH, N_EXPERTS, D_MODEL, 2 * D_EXPERT), D_MODEL ** -0.5),
        'w_expert_out': nrm(ks[20], (DEPTH, N_EXPERTS, D_EXPERT, D_MODEL), D_EXPERT ** -0.5),
        'g_final': 1.0 + nrm(ks[21], (D_MODEL,), 0.02),
    }

def reference(x_prompt, x_sample, cache_k, cache_v, cache_conv, meta_tokens,
              g_mix, w_in, conv_w, conv_b, conv_ln_g, conv_ln_b, g_sb, w_out,
              g_ffn, w_router_group, b_router_group, w_router_expert, b_router_expert,
              w_expert_in, w_expert_out, g_final):
    meta = jnp.broadcast_to(meta_tokens[None].astype(x_prompt.dtype), (x_prompt.shape[0], N_META, D_MODEL))
    xp = jnp.concatenate([meta, x_prompt], axis=1)
    xs = x_sample
    kp_l, vp_l, cp_l, ks_l, vs_l, cs_l = [], [], [], [], [], []
    for l in range(DEPTH):
        p = (g_mix[l], w_in[l], conv_w[l], conv_b[l], conv_ln_g[l], conv_ln_b[l], g_sb[l], w_out[l],
             g_ffn[l], w_router_group[l], b_router_group[l], w_router_expert[l], b_router_expert[l],
             w_expert_in[l], w_expert_out[l])
        zero_hist = jnp.zeros((xp.shape[0], CONV_WIDTH - 1, CONV_CH), xp.dtype)
        xp, kp, vp, cp = layer(xp, zero_hist, None, None, p)
        xs, ksn, vsn, csn = layer(xs, cache_conv[l], cache_k[l], cache_v[l], p)
        kp_l.append(kp); vp_l.append(vp); cp_l.append(cp)
        ks_l.append(ksn); vs_l.append(vsn); cs_l.append(csn)
    y_prompt = rmsnorm(xp, g_final)[:, N_META:]
    y_sample = rmsnorm(xs, g_final)
    new_k_prompt = jnp.stack(kp_l)
    new_v_prompt = jnp.stack(vp_l)
    new_conv_prompt = jnp.stack(cp_l)
    new_k_sample = jnp.stack(ks_l)
    new_v_sample = jnp.stack(vs_l)
    new_conv_sample = jnp.stack(cs_l)
    return (y_prompt, y_sample, new_k_prompt, new_v_prompt, new_conv_prompt,
            new_k_sample, new_v_sample, new_conv_sample)


_drawn_inputs = setup_inputs


def setup_inputs(seed=0):
    import zlib

    import numpy as np

    out = dict(_drawn_inputs(seed))
    spreads = {}
    factors = {'conv_ln_b': 3.663,
     'g_ffn': 2.726,
     'b_router_group': 8.0,
     'b_router_expert': 4.091,
     'g_final': 2.749}
    for name, (base, spread) in spreads.items():
        noise = np.random.default_rng([zlib.crc32(name.encode()), seed]).standard_normal(out[name].shape)
        drawn = base * np.exp(spread * noise) if base else spread * noise
        out[name] = __import__('jax').numpy.asarray(drawn.astype(out[name].dtype))
    for name, factor in factors.items():
        out[name] = (out[name] * factor).astype(out[name].dtype)
    return out
```

```python
from contextlib import ExitStack

import concourse.bass as bass
from concourse import mybir

ALU = mybir.AluOpType
ACT = mybir.ActivationFunctionType
AX = mybir.AxisListType
F32 = mybir.dt.float32
BF16 = mybir.dt.bfloat16
I32 = mybir.dt.int32
U32 = mybir.dt.uint32

P = 128
D = 1024
KD = D // P
CC = 512
NI = CC // P
HEADS, HD = 8, 64
META, SEQ, TS, PAST = 16, 512, 32, 1024
TP = META + SEQ
S0 = TP + 16
COLS = S0 + TS
HALF = COLS // 2
ROWS = [P, P, P, P, COLS - 4 * P]
NC = len(ROWS)
TAPS = 31
HIST = TAPS - 1
UW = HIST + TP + HIST + TS
US = HIST + TP
EPS = 1e-6
NEG = -1.0e30
ZCLAMP = 30.0
NG, EPG, NE, FE = 4, 8, 32, 256
TILE = 64
NTILE = COLS // TILE
BIGF = 65536.0
PAIRS = NE // 2
RING = 3
LN_VAR, LN_ROOT = 4, 7
LAG = 5
WSLOTS = 6


def build(nc, x_prompt, x_sample, cache_k, cache_v, cache_conv, meta, g_mix, w_in, conv_w, conv_b,
          ln_g, ln_b, g_sb, w_out, g_ffn, w_rg, b_rg, w_re, b_re, w_ei, w_eo, g_fin,
          y_p, y_s, nk_p, nv_p, ncv_p, nk_s, nv_s, ncv_s):
    with ExitStack() as ctx:
        def sb(name, shape, dt=F32):
            return ctx.enter_context(nc.sbuf_tensor(name, shape, dt))

        def sem(name):
            return ctx.enter_context(nc.semaphore(name))

        ps = ctx.enter_context(nc.psum_tensor("ps", [P, 8, 512], F32))

        x = sb("x", [P, NC, D])
        low = sb("low", [P, 14256])
        cw = sb("cw", [P, 8192])
        big = sb("big", [P, 4 * 6144])
        lowf = low[:, :]
        ht = lowf[:, 0:4608].rearrange("p (k t) -> p k t", k=KD)
        qk = lowf[:, 4608:9216].rearrange("p (k t) -> p k t", k=KD)
        vflat = lowf[:, 9216:11776]
        v = vflat.rearrange("p (c n) -> p c n", c=NC)
        uflat = lowf[:, 11776:14256]
        u = uflat.rearrange("p (i t) -> p i t", i=NI)

        ident = sb("ident", [P, P])
        ntri = sb("ntri", [P, P])
        nones = sb("nones", [P, P])
        identb = sb("identb", [P, P], BF16)
        negb = sb("negb", [P, P], BF16)
        tril = sb("tril", [P, P], BF16)
        onesb = sb("onesb", [P, P], BF16)
        vt = sb("vt", [P, 24])
        cwt = sb("cwt", [P, NI, TAPS])
        stat = sb("stat", [P, 48])
        stat_o = sb("stat_o", [P, NC * HEADS])
        nhalf = sb("nhalf", [P, 1])
        valid = sb("valid", [P, NC])
        bias36 = sb("bias36", [P, NG + NE])

        mixt = ht
        qt = qk[:, 0:NI, :]
        kt = qk[:, NI:2 * NI, :]
        h2t = qk
        ckt = cw[:, 0:4096].rearrange("p (i s) -> p i s", i=NI)
        cv = cw[:, 4096:8192].rearrange("p (b c) -> p b c", b=8)
        wout = cw[:, :].rearrange("p (k n) -> p k n", k=8)

        def part(lo, n):
            return big[:, lo:lo + n]

        win = [part(s * 1024, 1024).rearrange("p (k n) -> p k n", k=KD) for s in range(WSLOTS)]
        wv = part(6144, 4096).rearrange("p (k n) -> p k n", k=KD)
        ckraw = part(10240, 4096).rearrange("p (b c) -> p b c", b=8)
        conv = part(14336, 4 * (UW - HIST)).rearrange("p (i t) -> p i t", i=NI)
        yc = part(16704, NI * COLS).rearrange("p (i t) -> p i t", i=NI)
        ot = part(19008, NC * CC).rearrange("p (c n) -> p c n", c=NC)
        h1 = [part(21568 + 1024 * b, 1024) for b in range(2)]
        sgm = part(23616, COLS)
        vecrow = part(24192, P)
        lnsq = part(0, NI * COLS).rearrange("p (i t) -> p i t", i=NI)
        lnv = part(12288, COLS)
        lnt = part(12864, COLS)
        lnr = part(13440, COLS)
        convrow = part(10240, CC)
        histrow = part(10752, CC)
        sq1 = part(14336, D)
        za = [part(3072 + 512 * b, 512) for b in range(3)]
        el = [part(4608 + 512 * b, 512) for b in range(3)]
        wt = [part(6144 + 512 * b, 512) for b in range(3)]
        cs = [part(7680 + 512 * b, 512) for b in range(2)]
        ko = [part(8704 + 512 * b, 512) for b in range(2)]
        co = [part(9728, 512), part(10240, 512)]
        osq = part(10752, NC * CC).rearrange("p (c n) -> p c n", c=NC)
        h2 = [vflat[:, 0:1024], uflat[:, 0:1024]]
        gff = uflat[:, 1024:2048]
        sq2 = vflat[:, 1024:2048]
        wrt = vflat[:, 2048:2048 + KD * (NG + NE)].rearrange("p (k n) -> p k n", k=KD)
        slots = [part(6144 * q, 6144) for q in range(4)] + [lowf[:, 6144 * q:6144 * q + 6144] for q in range(2)]
        wi = [t[:, 0:4096].rearrange("p (k n) -> p k n", k=KD) for t in slots]
        wo = [t[:, 4096:6144].rearrange("p (k n) -> p k n", k=2) for t in slots]
        xg = [cw[:, 1024 * b:1024 * b + 1024] for b in range(3)]
        yg = [cw[:, 3072 + 1024 * b:4096 + 1024 * b] for b in range(3)]
        rest = lowf[:, 12288:14256]
        xt = [t.rearrange("p (k t) -> p k t", k=KD) for t in (cw[:, 6144:7168], cw[:, 7168:8192], rest[:, 0:1024])]
        sil = [rest[:, 1024 + 128 * b:1152 + 128 * b].rearrange("p (k t) -> p k t", k=2) for b in range(2)]
        act2 = [rest[:, 1280 + 128 * b:1408 + 128 * b].rearrange("p (k t) -> p k t", k=2) for b in range(2)]
        tab = rest[:, 1536:1536 + 4 * PAIRS].rearrange("p (g f) -> p g f", f=4)
        idx = [rest[:, 1600 + b:1601 + b].bitcast(I32) for b in range(3)]
        oidx = [rest[:, 1604 + b:1605 + b].bitcast(I32) for b in range(3)]
        gat = [rest[:, 1608 + b:1609 + b] for b in range(3)]
        more_tab = rest[0:TILE, 1612:1616]
        fill = cw[:, 0:576]

        def rt(lo, n):
            return cw[:, 1024 + lo:1024 + lo + n]

        lg = rt(0, NC * 36).rearrange("p (c n) -> p c n", c=NC)
        lm = rt(256, NC * NE)
        eqm = rt(512, NC * NE)
        o1 = rt(768, NC * NE)
        o2 = rt(1024, NC * NE)
        tmp = rt(1280, NC * NE)
        ex = rt(1536, NC * NE)
        io32 = rt(1792, NE)
        io4 = rt(1824, NG)
        colid = rt(1832, NC)
        gex = rt(1880, NC * NG)
        og = rt(1904, NC * NG)
        ent = [rt(1936 + 20 * b, 20).rearrange("p (c f) -> p c f", f=4) for b in range(2)]
        adr = [rt(1984 + 8 * b, NC).bitcast(I32) for b in range(2)]
        mb = rt(2000, 80).bitcast(BF16)
        sm = rt(2080, 128)
        ecol = rt(2208, NE)
        cnt = sb("cnt", [1, NE + 1], I32)
        y0 = [part(1024 * c, 1024) for c in range(NC)]
        y1 = [part(5120 + 1024 * c, 1024) for c in range(NC)]
        yo = [part(10240 + 1024 * c, 1024) for c in range(NC)]
        gfn = part(15360, 1024)
        sq3 = part(16384, 1024)

        h2_dram = nc.dram_tensor("h2_dram", (COLS, D), F32, kind="Internal").ap()
        tab_dram = nc.dram_tensor("tab_dram", (COLS * NE, 4), F32, kind="Internal").ap()
        y_dram = nc.dram_tensor("y_dram", (2 * COLS, D), F32, kind="Internal").ap()

        x_loaded = [sem(f"x_loaded{c}") for c in range(NC)]
        vec_loaded = sem("vec_loaded")
        convw_loaded = sem("convw_loaded")
        hist_loaded = sem("hist_loaded")
        win_loaded = [sem(f"win_loaded{s}") for s in range(WSLOTS)]
        wv_loaded = sem("wv_loaded")
        ck_loaded = sem("ck_loaded")
        cv_loaded = sem("cv_loaded")
        wout_loaded = sem("wout_loaded")
        router_loaded = sem("router_loaded")
        wi_loaded = [sem(f"wi_loaded{q}") for q in range(2 * RING)]
        wo_loaded = [sem(f"wo_loaded{q}") for q in range(2 * RING)]
        const_ready = sem("const_ready")
        pool_chain = sem("pool_chain")
        dve_chain = sem("dve_chain")
        act_chain = sem("act_chain")
        var_ready = sem("var_ready")
        rstd_ready = sem("rstd_ready")
        ssq_ready = sem("ssq_ready")
        h_ready = sem("h_ready")
        h_turned = sem("h_turned")
        ht_ready = sem("ht_ready")
        small_turned = sem("small_turned")
        small_ready = sem("small_ready")
        proj_done = sem("proj_done")
        sig_done = sem("sig_done")
        u_done = sem("u_done")
        qk_done = sem("qk_done")
        conv_done = sem("conv_done")
        yc_ready = sem("yc_ready")
        mean_done = sem("mean_done")
        dev_ready = sem("dev_ready")
        devsq_ready = sem("devsq_ready")
        var_done = sem("var_done")
        norm_ready = sem("norm_ready")
        ck_turned = sem("ck_turned")
        ckt_ready = sem("ckt_ready")
        v_done = sem("v_done")
        v_ready = sem("v_ready")
        even_done = sem("even_done")
        z_ready = sem("z_ready")
        zc_ready = sem("zc_ready")
        e_done = sem("e_done")
        l_done = sem("l_done")
        el_ready = sem("el_ready")
        cs_ready = sem("cs_ready")
        zr_ready = sem("zr_ready")
        w_ready = sem("w_ready")
        av_done = sem("av_done")
        o_ready = sem("o_ready")
        onorm_ready = sem("onorm_ready")
        o_turned = sem("o_turned")
        mixa_ready = sem("mixa_ready")
        mixb_ready = sem("mixb_ready")
        ko_turned = sem("ko_turned")
        ko_ready = sem("ko_ready")
        ko_stored = [sem(f"ko_stored{b}") for b in range(2)]
        co_turned = sem("co_turned")
        co_ready = sem("co_ready")
        small_stored = sem("small_stored")
        res_done = sem("res_done")
        x2_ready = sem("x2_ready")
        ssq2_ready = sem("ssq2_ready")
        h2_ready = sem("h2_ready")
        h2_turned = sem("h2_turned")
        h2t_ready = sem("h2t_ready")
        logit_done = sem("logit_done")
        h2_stored = [sem(f"h2_stored{b}") for b in range(2)]
        gsub_ready = sem("gsub_ready")
        gexp_ready = sem("gexp_ready")
        esub_ready = sem("esub_ready")
        eexp_ready = sem("eexp_ready")
        picks_ready = sem("picks_ready")
        pos_done = sem("pos_done")
        ent_ready = sem("ent_ready")
        tab_filled = sem("tab_filled")
        tab_stored = sem("tab_stored")
        tab_loaded = sem("tab_loaded")
        cnt_ready = sem("cnt_ready")
        zero_ready = sem("zero_ready")
        pe_passed = sem("pe_passed")
        pool_passed = sem("pool_passed")
        idx_ready = sem("idx_ready")
        gat_ready = sem("gat_ready")
        oidx_ready = sem("oidx_ready")
        gathered = [sem(f"gathered{b}") for b in range(3)]
        xg_turned = sem("xg_turned")
        xt_ready = sem("xt_ready")
        gu_done = sem("gu_done")
        sil_ready = sem("sil_ready")
        act_ready = sem("act_ready")
        y_done = sem("y_done")
        yg_ready = sem("yg_ready")
        scattered = [sem(f"scattered{b}") for b in range(3)]
        more_free = sem("more_free")
        more_loaded = sem("more_loaded")
        more_idx = sem("more_idx")
        more_gathered = sem("more_gathered")
        more_turned = sem("more_turned")
        more_xt = sem("more_xt")
        more_gu = sem("more_gu")
        more_sil = sem("more_sil")
        more_act = sem("more_act")
        more_rows = sem("more_rows")
        more_scaled = sem("more_scaled")
        more_scattered = sem("more_scattered")
        experts_done = sem("experts_done")
        y_loaded = [sem(f"y_loaded{c}") for c in range(NC)]
        gfn_loaded = sem("gfn_loaded")
        sum_ready = sem("sum_ready")
        ssq3_ready = sem("ssq3_ready")
        yo_ready = sem("yo_ready")
        yo_stored = sem("yo_stored")
        y01_ready = sem("y01_ready")
        lnl_done = sem("lnl_done")
        lnr_done = sem("lnr_done")
        lnv_ready = sem("lnv_ready")

        N_CONST = 18

        steps = []
        for unit, (q0, p0, blocks) in enumerate([(S0, 32, 9), (512, 0, 5)]):
            for n in range(blocks):
                own = n == 0
                b = blocks - 1 - n
                st = dict(unit=unit, n=HEADS * 32, first=own, last=n == blocks - 1,
                          rows=(p0, p0 + 32) if own else (0, P), q0=q0, p0=p0, b=b, own=own)
                steps.append(st)
        for h in range(HEADS):
            for b in range(3, -1, -1):
                steps.append(dict(unit=2 + h, h=h, b=b, n=512 - P * b, first=b == 3, last=b == 0,
                                  rows=(0, P)))
        NS = len(steps)
        sums = [sum(not st["last"] for st in steps[:s + 1]) for s in range(NS)]
        unit_bank = lambda unit: 6 + unit if unit < 2 else 4 + unit % 2

        block = ctx.enter_context(nc.Block())

        def pair_loop(eng, step, tail=0):
            for g in range(RING):
                step(g, g, 0)
            rounds = (PAIRS - tail) // RING
            with eng.Fori(1, rounds) as n:
                for s in range(RING):
                    step(n * RING + s, s, n)
            for g in range(rounds * RING, PAIRS):
                step(g, g % RING, g // RING)

        def peeled(g):
            return isinstance(g, int)

        def each_further_tile(eng, tile):
            eng.wait_ge(ent_ready, 1)
            most = eng.value_load(cnt[0:1, NE:NE + 1], min_val=0, max_val=COLS)
            with eng.If(most > TILE):
                n = eng.alloc_register("tiles")
                eng.reg_mov(n, 0)
                with eng.Fori(0, NE) as e:
                    tokens = eng.value_load(cnt[0:1, bass.ds(e, 1)], min_val=0, max_val=COLS)
                    with eng.If(tokens > TILE):
                        tiles = eng.snap((tokens + (TILE - 1)) // TILE, min_val=2, max_val=NTILE)
                        with eng.Fori(1, tiles) as t:
                            tile(eng.snap(n, min_val=0, max_val=2 * NTILE), e, t)
                            eng.reg_add(n, n, 1)

        @block.sync
        def _(sp):
            xp = x_prompt[0]
            sp.dma_start(x[0:META, 0, :], meta).then_inc(x_loaded[0], 16)
            sp.dma_start(x[META:P, 0, :], xp[0:P - META]).then_inc(x_loaded[0], 16)
            for r, g in enumerate((g_mix, conv_b, ln_g, ln_b, g_sb)):
                lo = 0 if r == 0 else 8 + 4 * (r - 1)
                k = 8 if r == 0 else 4
                sp.dma_start(vecrow[lo:lo + k, :], g[0].rearrange("(k n) -> k n", k=k)).then_inc(vec_loaded, 16)
            for c in range(1, 4):
                lo = P * c - META
                sp.dma_start(x[:, c, :], xp[lo:lo + P]).then_inc(x_loaded[c], 16)
            w3 = w_in[0].rearrange("(k p) n -> p k n", p=P)
            sp.dma_start(wv, w3[:, :, 4 * CC:5 * CC]).then_inc(wv_loaded, 16)
            sp.wait_ge(const_ready, 1)
            sp.dma_start(x[0:META, 4, :], xp[SEQ - META:SEQ]).then_inc(x_loaded[4], 16)
            sp.dma_start(x[32:64, 4, :], x_sample[0]).then_inc(x_loaded[4], 16)
            sp.dma_start(convrow[0:TAPS, :], conv_w[0]).then_inc(convw_loaded, 16)
            sp.dma_start(histrow[0:HIST, :], cache_conv[0, 0]).then_inc(hist_loaded, 16)
            starts = []
            for i in range(NI):
                starts += [CC + P * i, P * i]
            for i in range(NI):
                starts += [3 * CC + P * i, 2 * CC + P * i]
            for j, lo in enumerate(starts):
                if j >= WSLOTS:
                    sp.wait_ge(proj_done, j - WSLOTS + 1)
                sp.dma_start(win[j % WSLOTS], w3[:, :, lo:lo + P]).then_inc(win_loaded[j % WSLOTS], 16)
                if j == WSLOTS:
                    sp.wait_ge(small_ready, 3)
                    sp.dma_start(ckraw, cache_k[0, 0].rearrange("(b p) h d -> p b (h d)", p=P)).then_inc(ck_loaded, 16)
                    sp.dma_start(cv, cache_v[0, 0].rearrange("(b p) h d -> p b (h d)", p=P)).then_inc(cv_loaded, 16)
            for c in range(4):
                sp.wait_ge(v_ready, c + 1)
                sp.dma_start(nv_p[0, 0, P * c:P * c + P].rearrange("t h d -> t (h d)"), v[:, c, :]).then_inc(small_stored, 16)
            sp.wait_ge(v_ready, 5)
            sp.dma_start(nv_p[0, 0, 512:TP].rearrange("t h d -> t (h d)"), v[0:16, 4, :]).then_inc(small_stored, 16)
            sp.dma_start(nv_s[0, 0].rearrange("t h d -> t (h d)"), v[32:64, 4, :]).then_inc(small_stored, 16)
            sp.wait_ge(av_done, 9)
            sp.dma_start(wout, w_out[0].rearrange("(k p) n -> p k n", p=P)).then_inc(wout_loaded, 16)
            for c in range(NC):
                sp.wait_ge(ko_ready, c + 1)
                src = ko[c % 2]
                if c < 4:
                    sp.dma_start(nk_p[0, 0, P * c:P * c + P].rearrange("t h d -> t (h d)"), src).then_inc(ko_stored[c % 2], 16)
                else:
                    sp.dma_start(nk_p[0, 0, 512:TP].rearrange("t h d -> t (h d)"), src[0:16, :]).then_inc(ko_stored[c % 2], 16)
                    sp.dma_start(nk_s[0, 0].rearrange("t h d -> t (h d)"), src[32:64, :]).then_inc(ko_stored[c % 2], 16)
            sp.wait_ge(co_ready, 2)
            sp.dma_start(ncv_p[0, 0], co[0][0:HIST, :]).then_inc(small_stored, 16)
            sp.dma_start(ncv_s[0, 0], co[1][0:HIST, :]).then_inc(small_stored, 16)
            sp.wait_ge(mixa_ready, NI)
            sp.wait_ge(mixb_ready, NC)
            sp.wait_ge(ko_stored[0], 16 * 4)
            sp.wait_ge(ko_stored[1], 16 * 2)
            sp.wait_ge(small_stored, 16 * 8)
            sp.dma_start(wrt[:, :, 0:NG], w_rg[0].rearrange("(k p) n -> p k n", p=P)).then_inc(router_loaded, 16)
            sp.dma_start(wrt[:, :, NG:], w_re[0].rearrange("(k p) n -> p k n", p=P)).then_inc(router_loaded, 16)
            sp.dma_start(gff, g_ffn[0:1].broadcast_to([P, D])).then_inc(router_loaded, 16)
            sp.dma_start(bias36[:, 0:NG], b_rg[0:1].broadcast_to([P, NG])).then_inc(router_loaded, 16)
            sp.dma_start(bias36[:, NG:], b_re[0:1].broadcast_to([P, NE])).then_inc(router_loaded, 16)

            def load_wi(g, s, half):
                q = 2 * s + half
                if not peeled(g) or g >= RING:
                    sp.wait_ge(gu_done, (g - RING) * 2 + half + 1)
                e = bass.ds(g * 2 + half, 1)
                sp.dma_start(wi[q], w_ei[0, e].rearrange("a (k p) n -> p (a k) n", p=P)).then_inc(wi_loaded[q], 16)

            def load_wo(g, s):
                if not peeled(g) or g >= RING:
                    sp.wait_ge(y_done, g - RING + 1)
                for half in range(2):
                    q = 2 * s + half
                    e = bass.ds(g * 2 + half, 1)
                    sp.dma_start(wo[q], w_eo[0, e].rearrange("a (k p) n -> p (a k) n", p=P)).then_inc(wo_loaded[q], 16)

            load_wi(0, 0, 0)
            load_wi(0, 0, 1)
            for c in range(NC):
                sp.wait_ge(h2_ready, c + 1)
                sp.dma_start(h2_dram[P * c:P * c + ROWS[c], :], h2[c % 2][0:ROWS[c], :]).then_inc(h2_stored[c % 2], 16)
                if c == 0:
                    load_wo(0, 0)
                elif c < 3:
                    load_wi(1, 1, c - 1)
                elif c == 3:
                    load_wo(1, 1)
            sp.wait_ge(ent_ready, 1)
            sp.wait_ge(h2_stored[0], 16 * 3)
            sp.wait_ge(h2_stored[1], 16 * 2)
            sp.wait_ge(tab_stored, 16 * 2 * NC)
            for half in range(2):
                sp.dma_start(tab[TILE * half:TILE * half + TILE], tab_dram[0:TILE * NE, :].rearrange(
                    "(s h g) f -> h s g f", h=2, g=PAIRS)[half]).then_inc(tab_loaded, 16)
            sp.wait_ge(gathered[1], 16)
            load_wi(2, 2, 0)
            load_wi(2, 2, 1)

            def step(g, s):
                load_wi(g, s, 0)
                load_wo(g - 1, (s - 1) % RING)
                load_wi(g, s, 1)

            for g in range(RING, 2 * RING):
                step(g, g % RING)
            with sp.Fori(2, PAIRS // RING) as n:
                for s in range(RING):
                    step(n * RING + s, s)
            for g in range(PAIRS // RING * RING, PAIRS):
                step(g, g % RING)
            load_wo(PAIRS - 1, (PAIRS - 1) % RING)

            def more(n, e, t):
                sp.wait_ge(more_free, n + 1)
                sp.dma_start(more_tab, tab_dram[bass.ds(t * (TILE * NE), TILE * NE), :].rearrange(
                    "(s m) f -> s m f", m=NE)[:, bass.ds((e % 2) * PAIRS + e // 2, 1), :].rearrange(
                    "s m f -> s (m f)")).then_inc(more_loaded, 16)
                sp.dma_start(wi[0], w_ei[0, bass.ds(e, 1)].rearrange("a (k p) n -> p (a k) n", p=P)).then_inc(more_loaded, 16)
                sp.dma_start(wo[0], w_eo[0, bass.ds(e, 1)].rearrange("a (k p) n -> p (a k) n", p=P)).then_inc(more_loaded, 16)

            each_further_tile(sp, more)
            sp.wait_ge(experts_done, 1)
            sp.dma_start(gfn, g_fin.rearrange("(a d) -> a d", a=1).broadcast_to([P, D])).then_inc(gfn_loaded, 16)
            for c in range(NC):
                for k, dst in enumerate((y0[c], y1[c])):
                    lo = k * COLS + P * c
                    if c < 4:
                        sp.dma_start(dst, y_dram[lo:lo + P, :]).then_inc(y_loaded[c], 16)
                    else:
                        sp.dma_start(dst[0:16, :], y_dram[lo:lo + 16, :]).then_inc(y_loaded[c], 16)
                        sp.dma_start(dst[32:64, :], y_dram[lo + 32:lo + 64, :]).then_inc(y_loaded[c], 16)
            for c in range(NC):
                sp.wait_ge(yo_ready, c + 1)
                if c == 0:
                    sp.dma_start(y_p[0, 0:P - META], yo[c][META:P, :]).then_inc(yo_stored, 16)
                elif c < 4:
                    sp.dma_start(y_p[0, P * c - META:P * c + P - META], yo[c]).then_inc(yo_stored, 16)
                else:
                    sp.dma_start(y_p[0, SEQ - META:SEQ], yo[c][0:16, :]).then_inc(yo_stored, 16)
                    sp.dma_start(y_s[0], yo[c][32:64, :]).then_inc(yo_stored, 16)
            sp.wait_ge(yo_stored, 16 * 6)

        @block.gpsimd
        def _(pool):
            done = [0]

            def const(ins):
                done[0] += 1
                ins.then_inc(const_ready, 1)

            def settled():
                pool.wait_ge(const_ready, done[0])

            const(pool.memset(x[0:64, 4, :], 0.0))
            const(pool.memset(nhalf[:, :], -0.5))
            const(pool.memset(ident[:, :], 1.0))
            const(pool.memset(ntri[:, :], -1.0))
            const(pool.memset(nones[:, :], -1.0))
            const(pool.memset(identb[:, :], 1.0))
            const(pool.memset(negb[:, :], NEG))
            const(pool.memset(tril[:, :], 1.0))
            const(pool.memset(onesb[:, :], 1.0))
            const(pool.memset(u[:, :, 0:HIST], 0.0))
            const(pool.memset(valid[:, :], 1.0))
            const(pool.memset(yc[:, :, TP:S0], 0.0))
            settled()

            def keep(t, op, mult, fill=0.0):
                const(pool.affine_select(out=t, in_=t, pattern=[[-mult, P]], compare_op=op, fill=fill,
                                         base=0, channel_multiplier=mult))
            keep(ident[:, :], ALU.is_equal, 1)
            keep(ntri[:, :], ALU.is_ge, 1)
            keep(identb[:, :], ALU.is_equal, 1)
            keep(negb[:, :], ALU.is_ge, 1)
            keep(tril[:, :], ALU.is_gt, -1)
            const(pool.memset(valid[:, 4:5], 0.0))
            assert done[0] == N_CONST

            roots = [0]

            def root(t):
                roots[0] += 1
                pool.wait_ge(var_ready, roots[0])
                pool.tensor_tensor(t, t, nhalf[0:t.shape[0], :].broadcast_to(list(t.shape)), ALU.pow).then_inc(rstd_ready, 1)

            for c in range(NC):
                root(stat[0:ROWS[c], 24 + c:25 + c])

            pool.wait_ge(z_ready, 1)
            for s, st in enumerate(steps):
                r0, r1 = st["rows"]
                n = st["n"]
                if s >= 1:
                    pool.wait_ge(zr_ready, s)
                if st["last"]:
                    continue
                new, old = cs[s % 2], cs[(s - 1) % 2]
                if "h" in st:
                    c0 = P * st["b"]
                    pool.wait_ge(el_ready, s + 1)
                    if st["first"]:
                        pool.tensor_copy(new[:, c0:c0 + P], el[s % 3][:, 0:P]).then_inc(cs_ready, 1)
                    else:
                        pool.wait_ge(cs_ready, sums[s - 1])
                        pool.tensor_copy(new[:, c0:c0 + P], el[s % 3][:, 0:P])
                        pool.tensor_tensor(new[:, c0 + P:512], old[:, c0 + P:512], el[s % 3][:, P:n],
                                           ALU.add).then_inc(cs_ready, 1)
                elif st["first"]:
                    pool.memset(new[:, 0:n], 0.0).then_inc(pool_chain, 1)
                    pool.wait_ge(el_ready, s + 1)
                    pool.wait_ge(pool_chain, st["unit"] + 1)
                    pool.tensor_copy(new[r0:r1, 0:n], el[s % 3][r0:r1, 0:n]).then_inc(cs_ready, 1)
                else:
                    pool.wait_ge(el_ready, s + 1)
                    pool.wait_ge(cs_ready, sums[s - 1])
                    pool.tensor_tensor(new[:, 0:n], old[:, 0:n], el[s % 3][:, 0:n], ALU.add).then_inc(cs_ready, 1)

            root(stat_o[:, 0:4 * HEADS])
            root(stat_o[0:64, 4 * HEADS:5 * HEADS])
            for c in range(NC):
                root(stat[0:ROWS[c], 32 + c:33 + c])

            pool.wait_ge(res_done, NC)
            pool.memset(fill, BIGF).then_inc(zero_ready, 1)
            pool.iota(io32, [[1, NE]], base=0, channel_multiplier=0, allow_small_or_imprecise_dtypes=True).then_inc(zero_ready, 1)
            pool.iota(ecol, [[1, PAIRS], [PAIRS, 2]], base=0, channel_multiplier=0, allow_small_or_imprecise_dtypes=True).then_inc(zero_ready, 1)
            pool.iota(io4, [[1, NG]], base=0, channel_multiplier=0, allow_small_or_imprecise_dtypes=True).then_inc(zero_ready, 1)
            pool.iota(colid, [[P, NC]], base=0, channel_multiplier=1, allow_small_or_imprecise_dtypes=True).then_inc(zero_ready, 1)
            pool.memset(lg[:, 4, :], 0.0).then_inc(zero_ready, 1)
            pool.memset(ent[0], 0.0).then_inc(zero_ready, 1)
            pool.memset(ent[1], 0.0).then_inc(zero_ready, 1)
            pool.wait_ge(zero_ready, 1)
            pool.dma_start(tab_dram.rearrange("(p r) f -> p (r f)", p=P), fill).then_inc(tab_filled, 16)
            pool.wait_ge(tab_filled, 16)
            pool.wait_ge(ent_ready, 1)
            for k in range(2):
                for c in range(NC):
                    w = ROWS[c]
                    pool.indirect_dma_start(
                        out=tab_dram, out_offset=bass.IndirectOffsetOnAxis(ap=adr[k][0:w, c:c + 1].bitcast(U32), axis=0),
                        in_=ent[k][0:w, c, :], in_offset=None, bounds_check=COLS * NE - 1,
                        oob_is_err=False).then_inc(tab_stored, 16)
            pool.wait_ge(tab_loaded, 16 * 2)
            pool.wait_ge(h2_stored[0], 16 * 3)
            pool.wait_ge(h2_stored[1], 16 * 2)
            pool.memset(cw[:, 0:3072], 0.0).then_inc(pool_chain, 1)
            pool.wait_ge(pool_chain, 3)

            def gather(g, s):
                if not peeled(g) or g >= RING:
                    pool.wait_ge(xg_turned, g - RING + 1)
                pool.tensor_copy(idx[s], tab[:, bass.ds(g, 1), 0:1].rearrange("p a f -> p (a f)")).then_inc(idx_ready, 1)
                pool.wait_ge(idx_ready, g + 1)
                pool.sem_inc(pool_passed, 1)
                pool.indirect_dma_start(
                    out=xg[s], out_offset=None, in_=h2_dram,
                    in_offset=bass.IndirectOffsetOnAxis(ap=idx[s].bitcast(U32), axis=0),
                    bounds_check=COLS - 1, oob_is_err=False).then_inc(gathered[s], 16)

            def gates(g, s):
                if not peeled(g) or g >= RING:
                    pool.wait_ge(yg_ready, g - RING + 1)
                pool.tensor_copy(gat[s], tab[:, bass.ds(g, 1), 2:3].rearrange("p a f -> p (a f)")).then_inc(gat_ready, 1)

            def scatter(g, s, n):
                if not peeled(g) or g >= RING:
                    pool.wait_ge(scattered[s], n * 16)
                pool.tensor_copy(oidx[s], tab[:, bass.ds(g, 1), 1:2].rearrange("p a f -> p (a f)")).then_inc(oidx_ready, 1)
                pool.wait_ge(oidx_ready, g + 1)
                pool.wait_ge(yg_ready, g + 1)
                pool.sem_inc(pool_passed, 1)
                pool.indirect_dma_start(
                    out=y_dram, out_offset=bass.IndirectOffsetOnAxis(ap=oidx[s].bitcast(U32), axis=0),
                    in_=yg[s], in_offset=None, bounds_check=2 * COLS - 1,
                    oob_is_err=False).then_inc(scattered[s], 16)

            def step(g, s, n):
                gather(g, s)
                gates(g - LAG + RING, (s - LAG) % RING)
                scatter(g - LAG, (s - LAG) % RING, n - 2 if s < LAG - RING else n - 1)

            for g in range(RING):
                gather(g, g)
                gates(g, g)
            for g in range(RING, LAG):
                gather(g, g % RING)
            for g in range(LAG, 3 * RING):
                step(g, g % RING, g // RING)
            with pool.Fori(3, PAIRS // RING) as n:
                for s in range(RING):
                    step(n * RING + s, s, n)
            for g in range(PAIRS // RING * RING, PAIRS):
                step(g, g % RING, g // RING)
            for g in range(PAIRS - LAG, PAIRS):
                if g + RING < PAIRS:
                    gates(g + RING, g % RING)
                scatter(g, g % RING, g // RING)
            for b in range(3):
                pool.wait_ge(scattered[b], 16 * len(range(b, PAIRS, 3)))

            def more(n, e, t):
                pool.wait_ge(more_loaded, n * 48 + 48)
                pool.sem_inc(pool_passed, 1)
                pool.tensor_copy(idx[0][0:TILE], more_tab[:, 0:1]).then_inc(more_idx, 1)
                pool.tensor_copy(oidx[0][0:TILE], more_tab[:, 1:2]).then_inc(more_idx, 1)
                pool.wait_ge(more_idx, n * 2 + 2)
                pool.sem_inc(pool_passed, 1)
                pool.indirect_dma_start(
                    out=xg[0][0:TILE], out_offset=None, in_=h2_dram,
                    in_offset=bass.IndirectOffsetOnAxis(ap=idx[0][0:TILE].bitcast(U32), axis=0),
                    bounds_check=COLS - 1, oob_is_err=False).then_inc(more_gathered, 16)
                pool.wait_ge(more_scaled, n + 1)
                pool.sem_inc(pool_passed, 1)
                pool.indirect_dma_start(
                    out=y_dram, out_offset=bass.IndirectOffsetOnAxis(ap=oidx[0][0:TILE].bitcast(U32), axis=0),
                    in_=yg[0][0:TILE], in_offset=None, bounds_check=2 * COLS - 1,
                    oob_is_err=False).then_inc(more_scattered, 16)
                pool.wait_ge(more_scattered, n * 16 + 16)
                pool.sem_inc(more_free, 1)

            pool.sem_inc(more_free, 1)
            each_further_tile(pool, more)
            pool.sem_inc(experts_done, 1)
            for c in range(NC):
                w = ROWS[c]
                pool.wait_ge(y_loaded[c], 32 if c < 4 else 64)
                pool.tensor_tensor(y0[c][0:w, :], y0[c][0:w, :], y1[c][0:w, :], ALU.add).then_inc(y01_ready, 1)
                if c >= 1:
                    root(stat[0:ROWS[c - 1], 39 + c:40 + c])
            root(stat[0:ROWS[4], 44:45])

        @block.tensor
        def _(pe):
            pe.wait_ge(const_ready, N_CONST)
            pe.wait_ge(vec_loaded, 16 * 5)
            pe.transpose(ps[:, 4, 0:24], vecrow[0:24, :], ident[0:24, 0:24]).then_inc(small_turned, 1)
            def turn_input(c):
                w = ROWS[c]
                pe.wait_ge(h_ready, c + 1)
                if c >= 2:
                    pe.wait_ge(ht_ready, c - 1)
                pt = ps[:, 2 * (c % 2):2 * (c % 2) + 2, :].rearrange("p b (k t) -> p (b k) t", t=P)
                for k in range(KD):
                    mm = pe.transpose(pt[:, k, 0:w], h1[c % 2][0:w, P * k:P * k + P], ident[0:w, 0:w])
                mm.then_inc(h_turned, 1)

            def values(c):
                if c == 0:
                    pe.wait_ge(wv_loaded, 16)
                    pe.wait_ge(small_ready, 3)
                if c >= 2:
                    pe.wait_ge(v_ready, c - 1)
                w = ROWS[c]
                pe.wait_ge(ht_ready, c + 1)
                for k in range(KD):
                    mm = pe.matmul(ps[0:w, 4 + c % 2, :], ht[:, k, P * c:P * c + w], wv[:, k, :],
                                   start=k == 0, stop=k == KD - 1)
                mm.then_inc(v_done, 1)

            turn_input(0)
            pe.wait_ge(convw_loaded, 16)
            for i in range(NI):
                mm = pe.transpose(ps[:, 5, 31 * i:31 * i + 31], convrow[0:TAPS, P * i:P * i + P], ident[0:TAPS, 0:TAPS])
            mm.then_inc(small_turned, 1)
            pe.wait_ge(hist_loaded, 16)
            for i in range(NI):
                mm = pe.transpose(ps[:, 6, 30 * i:30 * i + 30], histrow[0:HIST, P * i:P * i + P], ident[0:HIST, 0:HIST])
            mm.then_inc(small_turned, 1)
            turn_input(1)
            for c in range(2, NC):
                values(c - 2)
                turn_input(c)
            values(3)
            values(4)
            pe.wait_ge(ht_ready, NC)
            for j in range(16):
                pe.wait_ge(win_loaded[j % WSLOTS], 16 * (j // WSLOTS + 1))
                if 2 <= j < 10 and j % 2 == 0:
                    pe.wait_ge(sig_done, (j - 2) // 2 + 1)
                elif 2 <= j < 10:
                    pe.wait_ge(u_done, (j - 3) // 2 + 1)
                elif j >= 10:
                    pe.wait_ge(qk_done, j - 9)
                for half in range(2):
                    for k in range(KD):
                        mm = pe.matmul(ps[:, 2 * (j % 2) + half, 0:HALF], win[j % WSLOTS][:, k, :],
                                       ht[:, k, HALF * half:HALF * half + HALF], start=k == 0, stop=k == KD - 1)
                mm.then_inc(proj_done, 1)
            pe.wait_ge(ck_loaded, 16)
            for b in range(8):
                if b >= 2:
                    pe.wait_ge(ckt_ready, b - 1)
                elif b == 0:
                    pe.wait_ge(small_ready, 3)
                for i in range(NI):
                    mm = pe.transpose(ps[:, 6 + b % 2, P * i:P * i + P], ckraw[:, b, P * i:P * i + P], ident[:, :])
                mm.then_inc(ck_turned, 1)
            pe.wait_ge(qk_done, 8)
            pe.wait_ge(yc_ready, 2 * NI)
            pe.wait_ge(v_ready, NC)
            for half in range(2):
                for i in range(NI):
                    mm = pe.matmul(ps[:, 4 + half, 0:HALF], nones[:, :], yc[:, i, HALF * half:HALF * half + HALF],
                                   start=i == 0, stop=i == NI - 1)
            mm.then_inc(mean_done, 1)
            def scores(s):
                st, z = steps[s], ps[:, s % 4, :]
                if s >= 4:
                    pe.wait_ge(w_ready, s - 3)
                if "h" in st:
                    i, r, b = st["h"] // 2, 64 * (st["h"] % 2), st["b"]
                    pe.matmul(z[:, 0:st["n"]], kt[r:r + 64, i, P * b:P * b + P], qt[r:r + 64, i, P * b:512],
                              start=True, stop=True)
                    pe.matmul(z[:, 0:P], identb[:, :], negb[:, :], start=False, stop=True,
                              skip_group_check=True).then_inc(z_ready, 1)
                    return
                q0, p0, (r0, r1) = st["q0"], st["p0"], st["rows"]
                for m, h in enumerate((0, 2, 4, 6, 1, 3, 5, 7)):
                    i, r = h // 2, 64 * (h % 2)
                    if m == 4:
                        mm.then_inc(even_done, 1)
                        pe.wait_ge(even_done, s + 1)
                    if st["own"]:
                        keys = kt[r:r + 64, i, q0:q0 + 32]
                    elif st["unit"] == 0:
                        keys = ckt[r:r + 64, i, P * st["b"]:P * st["b"] + P]
                    else:
                        keys = kt[r:r + 64, i, P * st["b"]:P * st["b"] + P]
                    mm = pe.matmul(z[r0:r1, 32 * h:32 * h + 32], keys, qt[r:r + 64, i, q0:q0 + 32],
                                   start=m == 0, stop=True, skip_group_check=True)
                if st["own"]:
                    for h in range(HEADS):
                        mm = pe.matmul(z[r0:r1, 32 * h:32 * h + 32], identb[r0:r1, r0:r1], negb[r0:r1, r0:r1],
                                       start=False, stop=True, skip_group_check=True)
                mm.then_inc(z_ready, 1)

            def reduce_later(s):
                st, z = steps[s], ps[:, s % 4, :]
                (r0, r1), n = st["rows"], st["n"]
                pe.wait_ge(el_ready, s + 1)
                if not st["first"]:
                    pe.wait_ge(cs_ready, sums[s - 1])
                    old = cs[(s - 1) % 2]
                    if "h" in st:
                        pe.matmul(z[:, P:n], nones[:, :], old[:, P * st["b"] + P:512], start=False, stop=True,
                                  skip_group_check=True)
                    else:
                        pe.matmul(z[:, 0:n], nones[:, :], old[:, 0:n], start=False, stop=True,
                                  skip_group_check=True)
                pe.matmul(z[r0:r1, 0:n], ntri[r0:r1, r0:r1], el[s % 3][r0:r1, 0:n], start=False, stop=True,
                          skip_group_check=True).then_inc(zr_ready, 1)

            def weigh(s):
                st = steps[s]
                w, o = wt[s % 3], ps[:, unit_bank(st["unit"]), :]
                (r0, r1), b = st["rows"], st["b"]
                if st["unit"] >= 4 and st["first"]:
                    pe.wait_ge(o_ready, st["unit"] - 1)
                if st["unit"] == 2 and st["first"]:
                    pe.wait_ge(norm_ready, NI)
                pe.wait_ge(w_ready, s + 1)
                if "h" in st:
                    h = st["h"]
                    for t in range(3, b - 1, -1):
                        mm = pe.matmul(o[:, 64 * t:64 * t + 64], w[:, P * (t - b):P * (t - b) + P],
                                       v[:, b, 64 * h:64 * h + 64], start=st["first"] and t == 3, stop=True,
                                       skip_group_check=True)
                else:
                    p0 = st["p0"]
                    for h in range(HEADS):
                        if st["own"]:
                            vals = v[r0:r1, 4, 64 * h:64 * h + 64]
                        elif st["unit"] == 0:
                            vals = cv[:, b, 64 * h:64 * h + 64]
                        else:
                            vals = v[:, b, 64 * h:64 * h + 64]
                        mm = pe.matmul(o[p0:p0 + 32, 64 * h:64 * h + 64], w[r0:r1, 32 * h:32 * h + 32], vals,
                                       start=st["first"] and h == 0, stop=True, skip_group_check=True)
                mm.then_inc(av_done, 1)

            def variance():
                pe.wait_ge(devsq_ready, NI)
                for half in range(2):
                    for i in range(NI):
                        mm = pe.matmul(ps[:, 4 + half, 0:HALF], nones[:, :],
                                       lnsq[:, i, HALF * half:HALF * half + HALF],
                                       start=i == 0, stop=i == NI - 1)
                mm.then_inc(var_done, 1)

            pe.wait_ge(ckt_ready, 8)
            pe.wait_ge(cv_loaded, 16)
            for s in range(NS + 3):
                if s < NS:
                    scores(s)
                if s == LN_VAR:
                    variance()
                if 2 <= s < NS + 2:
                    reduce_later(s - 2)
                if s >= 3:
                    weigh(s - 3)

            for c in range(NC):
                if c >= 2:
                    pe.wait_ge(ko_ready, c - 1)
                w = ROWS[c]
                for i in range(NI):
                    mm = pe.transpose(ps[0:w, 6 + c % 2, P * i:P * i + P], kt[:, i, P * c:P * c + w], ident[:, :])
                mm.then_inc(ko_turned, 1)
            pe.wait_ge(w_ready, NS)
            for b, lo in enumerate((US - HIST, US + TS)):
                for i in range(NI):
                    mm = pe.transpose(ps[0:HIST, b, P * i:P * i + P], u[:, i, lo:lo + HIST], ident[:, :])
                mm.then_inc(co_turned, 1)
            for c in range(NC):
                w = ROWS[c]
                if c == 0:
                    pe.wait_ge(onorm_ready, 1)
                else:
                    if c >= 2:
                        pe.wait_ge(mixb_ready, c - 1)
                for i in range(NI):
                    mm = pe.transpose(ps[:, 2 + c % 2, P * i:P * i + w], ot[0:w, c, P * i:P * i + P], ident[0:w, 0:w])
                mm.then_inc(o_turned, 1)
            pe.wait_ge(mixa_ready, NI)
            pe.wait_ge(mixb_ready, NC)
            pe.wait_ge(ko_ready, NC)
            pe.wait_ge(wout_loaded, 16)

            def project(c):
                w = ROWS[c]
                if c >= 2:
                    pe.wait_ge(x2_ready, c - 1)
                for n in range(2):
                    for k in range(KD):
                        mm = pe.matmul(ps[0:w, 4 + 2 * (c % 2) + n, :], mixt[:, k, P * c:P * c + w],
                                       wout[:, k, 512 * n:512 * n + 512], start=k == 0, stop=k == KD - 1)
                mm.then_inc(res_done, 1)

            def turn_h2(c):
                w = ROWS[c]
                pe.wait_ge(h2_ready, c + 1)
                if c >= 1:
                    pe.wait_ge(h2t_ready, c)
                else:
                    pe.wait_ge(co_ready, 2)
                pt = ps[:, 0:2, :].rearrange("p b (k t) -> p (b k) t", t=P)
                for k in range(KD):
                    mm = pe.transpose(pt[:, k, 0:w], h2[c % 2][0:w, P * k:P * k + P], ident[0:w, 0:w])
                mm.then_inc(h2_turned, 1)

            def logits(c):
                if c == 0:
                    pe.wait_ge(router_loaded, 16 * 5)
                    pe.wait_ge(mixb_ready, NC)
                w = ROWS[c]
                pe.wait_ge(h2t_ready, c + 1)
                for k in range(KD):
                    mm = pe.matmul(ps[0:w, 2, 36 * c:36 * c + 36], h2t[:, k, P * c:P * c + w], wrt[:, k, :],
                                   start=k == 0, stop=k == KD - 1, skip_group_check=True)
                mm.then_inc(logit_done, 1)

            for c in range(NC):
                project(c)
                if c >= 2:
                    turn_h2(c - 2)
                if c >= 3:
                    logits(c - 3)
            turn_h2(3)
            logits(2)
            turn_h2(4)
            logits(3)
            logits(4)
            pe.wait_ge(picks_ready, 1)
            for c in range(NC):
                for a in range(c + 1):
                    pe.matmul(ps[:, 3, NE * c:NE * c + NE], (tril if a == c else onesb)[:, :],
                              mb[:, NE * a:NE * a + NE], start=a == 0, stop=a == c, skip_group_check=True)
            for c in range(NC):
                mm = pe.matmul(ps[:, 3, NE * NC:NE * NC + NE], onesb[:, :], mb[:, NE * c:NE * c + NE],
                               start=c == 0, stop=c == NC - 1, skip_group_check=True)
            mm.then_inc(pos_done, 1)

            def turn(g, s, n):
                pe.wait_ge(gathered[s], n * 16 + 16)
                if not peeled(g) or g >= 1:
                    pe.wait_ge(xt_ready, g)
                for k in range(KD):
                    mm = pe.transpose(ps[:, k // 4, P * (k % 4):P * (k % 4) + P], xg[s][:, P * k:P * k + P], ident[:, :])
                mm.then_inc(xg_turned, 1)

            def gate_up(g, s, n, half):
                q = 2 * s + half
                pe.wait_ge(wi_loaded[q], n * 16 + 16)
                if half == 0:
                    pe.wait_ge(xt_ready, g + 1)
                if not peeled(g) or g >= 1:
                    pe.wait_ge(act_ready, g * 2 + half - 1)
                for m in range(4):
                    for k in range(KD):
                        mm = pe.matmul(ps[:, 2 + half, TILE * m:TILE * m + TILE], wi[q][:, k, P * m:P * m + P],
                                       xt[s][:, k, TILE * half:TILE * half + TILE],
                                       start=k == 0, stop=k == KD - 1, skip_group_check=True)
                mm.then_inc(gu_done, 1)

            def down(g, s, n):
                for half in range(2):
                    pe.wait_ge(wo_loaded[2 * s + half], n * 16 + 16)
                pe.wait_ge(act_ready, g * 2 + 2)
                if not peeled(g) or g >= 1:
                    pe.wait_ge(yg_ready, g)
                for m in range(2):
                    for k in range(2):
                        for half in range(2):
                            mm = pe.matmul(ps[TILE * half:TILE * half + TILE, 4 + m, :], act2[half][:, k, :],
                                           wo[2 * s + half][:, k, 512 * m:512 * m + 512], start=k == 0, stop=k == 1,
                                           skip_group_check=True)
                mm.then_inc(y_done, 1)

            def step(g, s, n):
                if not (peeled(g) and g == PAIRS - 1):
                    turn(g + 1, (s + 1) % RING, n if s + 1 < RING else n + 1)
                gate_up(g, s, n, 0)
                if not (peeled(g) and g == 0):
                    down(g - 1, (s - 1) % RING, n if s > 0 else n - 1)
                gate_up(g, s, n, 1)

            pe.wait_ge(ent_ready, 1)
            turn(0, 0, 0)
            pair_loop(pe, step, tail=1)
            down(PAIRS - 1, (PAIRS - 1) % RING, (PAIRS - 1) // RING)

            def more(n, e, t):
                pe.wait_ge(more_gathered, n * 16 + 16)
                pe.sem_inc(pe_passed, 1)
                for k in range(KD):
                    mm = pe.transpose(ps[:, k // 4, P * (k % 4):P * (k % 4) + TILE], xg[0][0:TILE, P * k:P * k + P],
                                      ident[0:TILE, 0:TILE])
                mm.then_inc(more_turned, 1)
                pe.wait_ge(more_xt, n + 1)
                pe.sem_inc(pe_passed, 1)
                for m in range(4):
                    for k in range(KD):
                        mm = pe.matmul(ps[:, 2, TILE * m:TILE * m + TILE], wi[0][:, k, P * m:P * m + P],
                                       xt[0][:, k, 0:TILE], start=k == 0, stop=k == KD - 1, skip_group_check=True)
                mm.then_inc(more_gu, 1)
                pe.wait_ge(more_act, n + 1)
                pe.sem_inc(pe_passed, 1)
                for m in range(2):
                    for k in range(2):
                        mm = pe.matmul(ps[0:TILE, 4 + m, :], act2[0][:, k, :], wo[0][:, k, 512 * m:512 * m + 512],
                                       start=k == 0, stop=k == 1)
                mm.then_inc(more_rows, 1)

            each_further_tile(pe, more)

        @block.scalar
        def _(act):
            def square_sum(out, src, acc):
                return act.activation(out, src, ACT.Square, accum_out=acc)

            def sumsq_input(c):
                w = ROWS[c]
                act.wait_ge(x_loaded[c], 32 if c in (0, 4) else 16)
                if c >= 1:
                    act.wait_ge(ssq_ready, c)
                square_sum(sq1[0:w, :], x[0:w, c, :], stat[0:w, c:c + 1]).then_inc(ssq_ready, 1)

            def copy_v(c):
                w = ROWS[c]
                act.wait_ge(v_done, c + 1)
                act.copy(v[0:w, c, :], ps[0:w, 4 + c % 2, :]).then_inc(v_ready, 1)

            act.wait_ge(small_turned, 1)
            act.copy(vt[:, :], ps[:, 4, 0:24]).then_inc(small_ready, 1)
            for c in range(NC):
                sumsq_input(c)
            act.wait_ge(small_turned, 2)
            act.copy(cwt[:, :, :], ps[:, 5, 0:NI * TAPS].rearrange("p (i j) -> p i j", i=NI)).then_inc(small_ready, 1)
            act.wait_ge(small_turned, 3)
            act.copy(u[:, :, US:US + HIST], ps[:, 6, 0:NI * HIST].rearrange("p (i j) -> p i j", i=NI)).then_inc(small_ready, 1)
            for c in range(NC):
                copy_v(c)
            for i in range(NI):
                act.wait_ge(proj_done, 2 * i + 1)
                if i >= 1:
                    act.wait_ge(u_done, i)
                act.activation(sgm.rearrange("p (a t) -> p a t", a=2), ps[:, 0:2, 0:HALF], ACT.Sigmoid).then_inc(sig_done, 1)
            for i in range(NI):
                act.wait_ge(proj_done, 9 + 2 * i)
                act.activation(kt[:, i, :].rearrange("p (a t) -> p a t", a=2), ps[:, 0:2, 0:HALF], ACT.Copy).then_inc(qk_done, 1)
                act.wait_ge(proj_done, 10 + 2 * i)
                act.activation(qt[:, i, :].rearrange("p (a t) -> p a t", a=2), ps[:, 2:4, 0:HALF], ACT.Copy,
                               scale=HD ** -0.5).then_inc(qk_done, 1)
            for b in range(8):
                act.wait_ge(ck_turned, b + 1)
                act.copy(ckt[:, :, P * b:P * b + P], ps[:, 6 + b % 2, :].rearrange("p (i t) -> p i t", i=NI)).then_inc(ckt_ready, 1)
            act.preload_act_table_set("natural_log_exp_and_others")

            def weights(s):
                st = steps[s]
                (r0, r1), n = st["rows"], st["n"]
                act.wait_ge(zr_ready, s + 1)
                if s >= 3:
                    act.wait_ge(av_done, s - 2)
                act.activation(wt[s % 3][r0:r1, 0:n], ps[r0:r1, s % 4, 0:n], ACT.Exp).then_inc(w_ready, 1)

            for s in range(NS + 2):
                if s < NS:
                    st = steps[s]
                    (r0, r1), n = st["rows"], st["n"]
                    a = za[s % 3][r0:r1, 0:n]
                    act.wait_ge(zc_ready, s + 1)
                    act.activation(a, a, ACT.Exp).then_inc(e_done, 1)
                if s == 1:
                    for i in range(NI):
                        act.wait_ge(dev_ready, i + 1)
                        act.square(lnsq[:, i, :], yc[:, i, :]).then_inc(devsq_ready, 1)
                if s == LN_ROOT:
                    act.wait_ge(lnv_ready, 1)
                    act.activation(lnr, lnv, ACT.Ln).then_inc(lnl_done, 1)
                    act.wait_ge(lnl_done, 1)
                    act.activation(lnr, lnr, ACT.Exp, scale=-0.5).then_inc(lnr_done, 1)
                if s >= 2:
                    weights(s - 2)
                if s < NS:
                    act.wait_ge(e_done, s + 1)
                    act.activation(a, a, ACT.Ln, bias=1.0).then_inc(l_done, 1)

            for i in range(NI):
                act.wait_ge(norm_ready, i + 1)
                act.activation(mixt[:, i, :], yc[:, i, :], ACT.Silu, bias=vt[:, 16 + i:17 + i],
                               scale=vt[:, 12 + i:13 + i]).then_inc(mixa_ready, 1)
            for c in range(NC):
                w = ROWS[c]
                act.wait_ge(ko_turned, c + 1)
                if c >= 2:
                    act.wait_ge(ko_stored[c % 2], 16 * (c // 2))
                act.copy(ko[c % 2][0:w, :], ps[0:w, 6 + c % 2, :]).then_inc(ko_ready, 1)
            for b in range(2):
                act.wait_ge(co_turned, b + 1)
                act.copy(co[b][0:HIST, :], ps[0:HIST, b, :]).then_inc(co_ready, 1)

            def copy_h2t(c):
                w = ROWS[c]
                act.wait_ge(h2_turned, c + 1)
                act.copy(h2t[:, :, P * c:P * c + w],
                         ps[:, 0:2, :].rearrange("p b (k t) -> p (b k) t", t=P)[:, :, 0:w]).then_inc(h2t_ready, 1)

            for c in range(NC):
                w = ROWS[c]
                act.wait_ge(x2_ready, c + 1)
                if c >= 1:
                    act.wait_ge(ssq2_ready, c)
                square_sum(sq2[0:w, :], x[0:w, c, :], stat[0:w, 8 + c:9 + c]).then_inc(ssq2_ready, 1)
                if c >= 2:
                    copy_h2t(c - 2)
            copy_h2t(3)
            copy_h2t(4)
            act.wait_ge(gsub_ready, 1)
            act.activation(gex, gex, ACT.Exp).then_inc(gexp_ready, 1)
            act.wait_ge(esub_ready, 1)
            act.activation(ex, ex, ACT.Exp).then_inc(eexp_ready, 1)

            def silu(g, half):
                act.wait_ge(gu_done, g * 2 + half + 1)
                if not peeled(g) or g >= 1:
                    act.wait_ge(act_ready, g * 2 + half - 1)
                act.activation(sil[half], ps[:, 2 + half, 0:2 * TILE].rearrange("p (k t) -> p k t", k=2),
                               ACT.Silu).then_inc(sil_ready, 1)

            def gated_rows(g, s, n):
                act.wait_ge(y_done, g + 1)
                act.wait_ge(gat_ready, g + 1)
                if not peeled(g) or g >= RING:
                    act.wait_ge(scattered[s], n * 16)
                act.activation(yg[s].rearrange("p (m n) -> p m n", m=2), ps[:, 4:6, :],
                               ACT.Copy, scale=gat[s]).then_inc(yg_ready, 1)

            def step(g, s, n):
                silu(g, 0)
                if not (peeled(g) and g == 0):
                    gated_rows(g - 1, (s - 1) % RING, n if s > 0 else n - 1)
                silu(g, 1)

            pair_loop(act, step, tail=1)
            gated_rows(PAIRS - 1, (PAIRS - 1) % RING, (PAIRS - 1) // RING)

            def more(n, e, t):
                act.wait_ge(more_gu, n + 1)
                act.activation(sil[0], ps[:, 2, 0:2 * TILE].rearrange("p (k t) -> p k t", k=2), ACT.Silu).then_inc(more_sil, 1)
                act.wait_ge(more_rows, n + 1)
                act.activation(yg[0][0:TILE].rearrange("p (m n) -> p m n", m=2), ps[0:TILE, 4:6, :], ACT.Copy,
                               scale=more_tab[:, 2:3]).then_inc(more_scaled, 1)

            each_further_tile(act, more)

            for c in range(NC):
                w = ROWS[c]
                act.wait_ge(sum_ready, c + 1)
                if c >= 1:
                    act.wait_ge(ssq3_ready, c)
                square_sum(sq3[0:w, :], x[0:w, c, :], stat[0:w, 16 + c:17 + c]).then_inc(ssq3_ready, 1)

        @block.vector
        def _(dve):
            chain = [0]
            rooted = [0]

            def halves(t):
                return t.rearrange("p (a t) -> p a t", a=2)

            def link(ins):
                chain[0] += 1
                ins.then_inc(dve_chain, 1)
                dve.wait_ge(dve_chain, chain[0])

            def rstd(dst, src, scale):
                dve.tensor_scalar(dst, src, scale, EPS, ALU.mult, ALU.add).then_inc(var_ready, 1)
                rooted[0] += 1
                dve.wait_ge(rstd_ready, rooted[0])

            def scale_input(c):
                w = ROWS[c]
                dve.wait_ge(ssq_ready, c + 1)
                rstd(stat[0:w, 24 + c:25 + c], stat[0:w, c:c + 1], 1.0 / D)
                if c >= 2:
                    dve.wait_ge(h_turned, c - 1)
                dve.tensor_scalar(h1[c % 2][0:w, :], x[0:w, c, :], stat[0:w, 24 + c:25 + c], None,
                                  ALU.mult).then_inc(h_ready, 1)

            def copy_ht(c):
                w = ROWS[c]
                dve.wait_ge(h_turned, c + 1)
                pt = ps[:, 2 * (c % 2):2 * (c % 2) + 2, :].rearrange("p b (k t) -> p (b k) t", t=P)
                dve.tensor_tensor(ht[:, :, P * c:P * c + w], pt[:, :, 0:w],
                                  vt[:, 0:KD].unsqueeze(2).broadcast_to([P, KD, w]), ALU.mult).then_inc(ht_ready, 1)

            scale_input(0)
            scale_input(1)
            dve.wait_ge(small_ready, 1)
            for c in range(NC):
                copy_ht(c)
                if c + 2 < NC:
                    scale_input(c + 2)

            CW = UW - HIST

            def tap(i, j):
                if j == 0:
                    link(dve.tensor_scalar(conv[:, i, :], u[:, i, 0:CW], cwt[:, i, 0:1], None, ALU.mult))
                else:
                    link(dve.scalar_tensor_tensor(conv[:, i, :], u[:, i, j:j + CW], cwt[:, i, j:j + 1],
                                                  conv[:, i, :], ALU.mult, ALU.add))
                if j == TAPS - 1:
                    for dst, src in ((yc[:, i, 0:TP], conv[:, i, 0:TP]), (yc[:, i, S0:COLS], conv[:, i, US:US + TS])):
                        dve.tensor_scalar(dst, src, vt[:, 8 + i:9 + i], None, ALU.add).then_inc(yc_ready, 1)

            taps = [(i, j) for i in range(NI) for j in range(TAPS)]
            dve.wait_ge(small_ready, 3)
            for i in range(NI):
                dve.wait_ge(proj_done, 2 * i + 2)
                dve.wait_ge(sig_done, i + 1)
                dve.tensor_tensor(u[:, i, HIST:HIST + HALF], ps[:, 2, 0:HALF], sgm[:, 0:HALF], ALU.mult).then_inc(conv_done, 1)
                dve.tensor_tensor(u[:, i, HIST + HALF:HIST + TP], ps[:, 3, 0:TP - HALF], sgm[:, HALF:TP], ALU.mult).then_inc(conv_done, 1)
                dve.tensor_tensor(u[:, i, UW - TS:UW], ps[:, 3, S0 - HALF:HALF], sgm[:, S0:COLS], ALU.mult).then_inc(u_done, 1)
                dve.wait_ge(conv_done, 2 * i + 2)
                dve.wait_ge(u_done, i + 1)
                for _ in range(18 if i < NI - 1 else len(taps)):
                    tap(*taps.pop(0))

            def deviations():
                dve.wait_ge(mean_done, 1)
                dve.wait_ge(yc_ready, 2 * NI)
                for i in range(NI):
                    dve.scalar_tensor_tensor(halves(yc[:, i, :]), ps[:, 4:6, 0:HALF], 1.0 / CC,
                                             halves(yc[:, i, :]), ALU.mult, ALU.add).then_inc(dev_ready, 1)

            def variances():
                dve.wait_ge(var_done, 1)
                dve.tensor_scalar(halves(lnv), ps[:, 4:6, 0:HALF], -1.0 / CC, EPS, ALU.mult, ALU.add).then_inc(lnv_ready, 1)

            def layer_norm():
                dve.wait_ge(lnr_done, 1)
                dve.wait_ge(lnv_ready, 1)
                link(dve.tensor_tensor(lnt, lnr, lnr, ALU.mult))
                link(dve.tensor_tensor(lnt, lnt, lnv, ALU.mult))
                link(dve.tensor_scalar(lnt, lnt, -0.5, 1.5, ALU.mult, ALU.add))
                link(dve.tensor_tensor(lnr, lnr, lnt, ALU.mult))
                dve.wait_ge(dev_ready, NI)
                for i in range(NI):
                    dve.tensor_tensor(yc[:, i, :], yc[:, i, :], lnr, ALU.mult).then_inc(norm_ready, 1)

            def clamp(s):
                st = steps[s]
                (r0, r1), n = st["rows"], st["n"]
                dve.wait_ge(z_ready, s + 1)
                if s >= 3:
                    dve.wait_ge(el_ready, s - 2)
                dve.tensor_scalar(za[s % 3][r0:r1, 0:n], ps[r0:r1, s % 4, 0:n], ZCLAMP, None, ALU.min).then_inc(zc_ready, 1)

            def softplus(s):
                st = steps[s]
                (r0, r1), n = st["rows"], st["n"]
                dve.wait_ge(l_done, s + 1)
                if s >= 3:
                    dve.wait_ge(zr_ready, s - 2)
                    dve.wait_ge(cs_ready, sums[s - 3])
                dve.tensor_tensor(el[s % 3][r0:r1, 0:n], ps[r0:r1, s % 4, 0:n], za[s % 3][r0:r1, 0:n],
                                  ALU.max).then_inc(el_ready, 1)

            def unit_out(s):
                st = steps[s]
                if not st["last"]:
                    return
                dve.wait_ge(av_done, s + 1)
                o = ps[:, unit_bank(st["unit"]), :]
                if "h" in st:
                    h = st["h"]
                    dve.tensor_copy(ot[:, 0:4, 64 * h:64 * h + 64],
                                    o[:, 0:256].rearrange("p (t d) -> p t d", t=4)).then_inc(o_ready, 1)
                else:
                    p0 = st["p0"]
                    dve.tensor_copy(ot[p0:p0 + 32, 4, :], o[p0:p0 + 32, :]).then_inc(o_ready, 1)

            for s in range(NS + 4):
                if s < NS:
                    clamp(s)
                if s == 0:
                    deviations()
                if s == LN_ROOT - 1:
                    variances()
                if s == LN_ROOT + 1:
                    layer_norm()
                if 1 <= s <= NS:
                    softplus(s - 1)
                if s >= 4:
                    unit_out(s - 4)
            dve.wait_ge(o_ready, 2 + HEADS)
            q = 0
            for lo, w, cc in ((0, P, slice(0, 4)), (0, 64, slice(4, 5))):
                k = cc.stop - cc.start
                link(dve.tensor_tensor(osq[0:w, cc, :], ot[0:w, cc, :], ot[0:w, cc, :], ALU.mult))
                st8 = stat_o[0:w, q:q + k * HEADS]
                link(dve.tensor_reduce(st8, osq[0:w, cc, :].rearrange("p c (h d) -> p (c h) d", d=HD), AX.X, ALU.add))
                rstd(st8, st8, 1.0 / HD)
                o4 = ot[0:w, cc, :].rearrange("p c (h d) -> p (c h) d", d=HD)
                ins = dve.tensor_tensor(o4, o4, st8.unsqueeze(2).broadcast_to([w, k * HEADS, HD]), ALU.mult)
                q += k * HEADS
                if q < NC * HEADS:
                    link(ins)
                else:
                    ins.then_inc(onorm_ready, 1)
            for c in range(NC):
                w = ROWS[c]
                dve.wait_ge(o_turned, c + 1)
                dve.tensor_tensor(mixt[:, NI:2 * NI, P * c:P * c + w],
                                  ps[:, 2 + c % 2, :].rearrange("p (i t) -> p i t", i=NI)[:, :, 0:w],
                                  vt[:, 20:24].unsqueeze(2).broadcast_to([P, NI, w]), ALU.mult).then_inc(mixb_ready, 1)

            dve.wait_ge(router_loaded, 16 * 5)
            for c in range(NC):
                w = ROWS[c]
                dve.wait_ge(res_done, c + 1)
                dve.tensor_tensor(x[0:w, c, :].rearrange("p (a n) -> p a n", a=2), x[0:w, c, :].rearrange("p (a n) -> p a n", a=2),
                                  ps[0:w, 4 + 2 * (c % 2):6 + 2 * (c % 2), :], ALU.add).then_inc(x2_ready, 1)
                dve.wait_ge(ssq2_ready, c + 1)
                rstd(stat[0:w, 32 + c:33 + c], stat[0:w, 8 + c:9 + c], 1.0 / D)
                if c >= 2:
                    dve.wait_ge(h2_turned, c - 1)
                    dve.wait_ge(h2_stored[c % 2], 16 * (c // 2))
                dve.scalar_tensor_tensor(h2[c % 2][0:w, :], x[0:w, c, :], stat[0:w, 32 + c:33 + c], gff[0:w, :],
                                         ALU.mult, ALU.mult).then_inc(h2_ready, 1)

            def v5(k):
                return sm[:, 5 * k:5 * k + 5]

            def wide(t, n):
                return t.unsqueeze(2).broadcast_to([P, NC, n])

            def over(t, n):
                return t.unsqueeze(1).broadcast_to([P, NC, n])

            def c3(t):
                return t.rearrange("p (c n) -> p c n", c=NC)

            gmax, gsum, m1, m2, esum, e2, first, t0, t1, pg, p1, p2 = (v5(k) for k in range(12))
            dve.wait_ge(router_loaded, 16 * 5)
            dve.wait_ge(zero_ready, 8)
            dve.wait_ge(logit_done, NC)
            for c in range(NC):
                w = ROWS[c]
                link(dve.tensor_tensor(lg[0:w, c, :], ps[0:w, 2, 36 * c:36 * c + 36], bias36[0:w, :], ALU.add))
            lgg = lg[:, :, 0:NG]
            lge = lg[:, :, NG:NG + NE]
            link(dve.tensor_reduce(gmax, lgg, AX.X, ALU.max))
            dve.tensor_tensor(c3(gex), lgg, wide(gmax, NG), ALU.subtract).then_inc(gsub_ready, 1)

            def first_of(dst, src, top, iota, n, scratch):
                link(dve.tensor_tensor(c3(scratch), src, wide(top, n), ALU.is_equal))
                link(dve.scalar_tensor_tensor(c3(scratch), c3(scratch), -1000.0, over(iota, n), ALU.mult, ALU.add))
                link(dve.tensor_reduce(first, c3(scratch), AX.X, ALU.min))
                link(dve.tensor_tensor(c3(dst), c3(scratch), wide(first, n), ALU.is_equal))

            first_of(og, lgg, gmax, io4, NG, tmp[:, 0:NC * NG])
            link(dve.tensor_scalar(og, og, -NEG, NEG, ALU.mult, ALU.add))
            link(dve.tensor_tensor(lm.rearrange("p (c g e) -> p c g e", c=NC, g=NG), lge.rearrange("p c (g e) -> p c g e", g=NG),
                                   c3(og).unsqueeze(3).broadcast_to([P, NC, NG, EPG]), ALU.add))
            link(dve.tensor_reduce(m1, c3(lm), AX.X, ALU.max))
            dve.tensor_tensor(c3(ex), c3(lm), wide(m1, NE), ALU.subtract).then_inc(esub_ready, 1)
            first_of(o1, c3(lm), m1, io32, NE, eqm)
            link(dve.scalar_tensor_tensor(eqm, o1, 2 * NEG, lm, ALU.mult, ALU.add))
            link(dve.tensor_reduce(m2, c3(eqm), AX.X, ALU.max))
            first_of(o2, c3(eqm), m2, io32, NE, tmp)
            link(dve.memset(valid[0:64, 4:5], 1.0))
            link(dve.tensor_scalar(t0, colid, float(TP), None, ALU.is_lt))
            link(dve.tensor_scalar(t1, colid, float(S0), None, ALU.is_ge))
            link(dve.tensor_tensor(t0, t0, t1, ALU.add))
            link(dve.tensor_tensor(valid[:, :], valid[:, :], t0, ALU.mult))
            link(dve.tensor_tensor(c3(o1), c3(o1), wide(valid[:, :], NE), ALU.mult))
            link(dve.tensor_tensor(c3(o2), c3(o2), wide(valid[:, :], NE), ALU.mult))
            dve.tensor_tensor(mb, o1, o2, ALU.add).then_inc(picks_ready, 1)
            dve.wait_ge(gexp_ready, 1)
            link(dve.tensor_reduce(gsum, c3(gex), AX.X, ALU.add))
            link(dve.reciprocal(pg, gsum))
            dve.wait_ge(eexp_ready, 1)
            link(dve.tensor_reduce(esum, c3(ex), AX.X, ALU.add))
            link(dve.tensor_tensor(tmp, ex, o2, ALU.mult))
            link(dve.tensor_reduce(e2, c3(tmp), AX.X, ALU.add))
            link(dve.reciprocal(p1, esum))
            link(dve.tensor_tensor(p2, e2, p1, ALU.mult))
            link(dve.tensor_tensor(t0, p1, p2, ALU.add))
            link(dve.reciprocal(t0, t0))
            link(dve.tensor_tensor(t0, t0, pg, ALU.mult))
            link(dve.tensor_tensor(ent[0][:, :, 2], p1, t0, ALU.mult))
            link(dve.tensor_tensor(ent[1][:, :, 2], p2, t0, ALU.mult))
            for k in range(2):
                link(dve.tensor_copy(ent[k][:, :, 0], colid))
                link(dve.tensor_scalar(ent[k][:, :, 1], colid, float(COLS * k), None, ALU.add))
            link(dve.tensor_scalar(t1, valid[:, :], -BIGF, BIGF, ALU.mult, ALU.add))
            dve.wait_ge(pos_done, 1)
            pos = ps[:, 3, 0:NC * NE]
            for k, o in enumerate((o1, o2)):
                link(dve.scalar_tensor_tensor(c3(tmp), c3(pos), float(NE), over(ecol, NE), ALU.mult, ALU.add))
                link(dve.tensor_tensor(tmp, tmp, o, ALU.mult))
                link(dve.tensor_reduce(t0, c3(tmp), AX.X, ALU.add))
                link(dve.tensor_tensor(adr[k], t0, t1, ALU.add))
            link(dve.tensor_reduce(sm[0:1, 100:101], ps[0:1, 3, NE * NC:NE * NC + NE], AX.X, ALU.max))
            link(dve.tensor_copy(cnt[:, 0:NE], ps[0:1, 3, NE * NC:NE * NC + NE]))
            dve.tensor_copy(cnt[:, NE:NE + 1], sm[0:1, 100:101]).then_inc(ent_ready, 1)

            def copy_xt(g, s):
                dve.wait_ge(xg_turned, g + 1)
                if not peeled(g) or g >= RING:
                    dve.wait_ge(gu_done, (g - RING) * 2 + 2)
                dve.tensor_copy(xt[s], ps[:, 0:2, :].rearrange("p b (k t) -> p (b k) t", t=P)).then_inc(xt_ready, 1)

            def gate_times_up(g, half):
                dve.wait_ge(sil_ready, g * 2 + half + 1)
                if not peeled(g) or g >= 1:
                    dve.wait_ge(y_done, g)
                dve.tensor_tensor(act2[half], sil[half], ps[:, 2 + half, 2 * TILE:4 * TILE].rearrange("p (k t) -> p k t", k=2),
                                  ALU.mult).then_inc(act_ready, 1)

            def step(g, s, n):
                if not (peeled(g) and g == PAIRS - 1):
                    copy_xt(g + 1, (s + 1) % RING)
                for half in range(2):
                    gate_times_up(g, half)

            dve.wait_ge(tab_loaded, 32)
            copy_xt(0, 0)
            pair_loop(dve, step, tail=1)

            def more(n, e, t):
                dve.wait_ge(more_turned, n + 1)
                dve.tensor_copy(xt[0][:, :, 0:TILE], ps[:, 0:2, :].rearrange("p b (k t) -> p (b k) t", t=P)[:, :, 0:TILE]).then_inc(more_xt, 1)
                dve.wait_ge(more_sil, n + 1)
                dve.tensor_tensor(act2[0], sil[0], ps[:, 2, 2 * TILE:4 * TILE].rearrange("p (k t) -> p k t", k=2),
                                  ALU.mult).then_inc(more_act, 1)

            each_further_tile(dve, more)

            def add_experts(c):
                w = ROWS[c]
                dve.wait_ge(y01_ready, c + 1)
                dve.tensor_tensor(x[0:w, c, :], x[0:w, c, :], y0[c][0:w, :], ALU.add).then_inc(sum_ready, 1)

            def norm_out(c):
                w = ROWS[c]
                dve.wait_ge(ssq3_ready, c + 1)
                rstd(stat[0:w, 40 + c:41 + c], stat[0:w, 16 + c:17 + c], 1.0 / D)
                dve.scalar_tensor_tensor(yo[c][0:w, :], x[0:w, c, :], stat[0:w, 40 + c:41 + c], gfn[0:w, :],
                                         ALU.mult, ALU.mult).then_inc(yo_ready, 1)

            dve.wait_ge(gfn_loaded, 16)
            for c in range(NC + 1):
                if c < NC:
                    add_experts(c)
                if c >= 1:
                    norm_out(c - 1)


_INS = ['x_prompt', 'x_sample', 'cache_k', 'cache_v', 'cache_conv', 'meta_tokens', 'g_mix', 'w_in',
        'conv_w', 'conv_b', 'conv_ln_g', 'conv_ln_b', 'g_sb', 'w_out', 'g_ffn', 'w_router_group',
        'b_router_group', 'w_router_expert', 'b_router_expert', 'w_expert_in', 'w_expert_out', 'g_final']
_OUTS = [(1, SEQ, D), (1, TS, D), (1, 1, TP, HEADS, HD), (1, 1, TP, HEADS, HD), (1, 1, HIST, CC),
         (1, 1, TS, HEADS, HD), (1, 1, TS, HEADS, HD), (1, 1, HIST, CC)]


def kernel(**inputs):
    import numpy as _np
    import concourse.bacc as _bacc
    from concourse import mybir as _mybir
    from concourse.bass_utils import run_bass_kernel_spmd as _run

    nc = _bacc.Bacc("TRN2", target_bir_lowering=False, num_devices=1)
    arrays, args = {}, []
    for name in _INS:
        a = _np.ascontiguousarray(inputs[name])
        arrays[f"in_{name}"] = a
        args.append(nc.dram_tensor(f"in_{name}", a.shape, _mybir.dt.from_np(a.dtype), kind="ExternalInput").ap())
    for i, shape in enumerate(_OUTS):
        args.append(nc.dram_tensor(f"out_{i}", shape, _mybir.dt.float32, kind="ExternalOutput").ap())
    build(nc, *args)
    r = _run(nc, [arrays], core_ids=[0])
    return tuple(r.results[0][f"out_{i}"] for i in range(len(_OUTS)))
```

```python
from contextlib import ExitStack

import concourse.bass as bass
from concourse import mybir

ALU = mybir.AluOpType
ACT = mybir.ActivationFunctionType
AX = mybir.AxisListType
F32 = mybir.dt.float32
F32R = mybir.dt.float32r
BF16 = mybir.dt.bfloat16
I32 = mybir.dt.int32
U32 = mybir.dt.uint32

P = 128
D = 1024
KD = D // P
CC = 512
NI = CC // P
HEADS, HD = 8, 64
META, SEQ, TS, PAST = 16, 512, 32, 1024
TP = META + SEQ
S0 = TP + 16
COLS = S0 + TS
HALF = COLS // 2
ROWS = [P, P, P, P, COLS - 4 * P]
NC = len(ROWS)
TAPS = 31
HIST = TAPS - 1
UW = HIST + TP + HIST + TS
US = HIST + TP
EPS = 1e-6
NEG = -1.0e30
ZCLAMP = 30.0
NG, EPG, NE, FE = 4, 8, 32, 256
TILE = 64
NTILE = COLS // TILE
BIGF = 65536.0
PAIRS = NE // 2
RING = 3
TAPS_EARLY = (13, 13, 13, 50)
TAPS_STEP = 2
LN_STEP = 24
LAG = 5
POOL_ADDS = (0,)
POOL_NORMS = (0, 1)
WSLOTS = 6
WARM = 12
HSLOTS = 3


def build(nc, x_prompt, x_sample, cache_k, cache_v, cache_conv, meta, g_mix, w_in, conv_w, conv_b,
          ln_g, ln_b, g_sb, w_out, g_ffn, w_rg, b_rg, w_re, b_re, w_ei, w_eo, g_fin,
          y_p, y_s, nk_p, nv_p, ncv_p, nk_s, nv_s, ncv_s):
    with ExitStack() as ctx:
        def sb(name, shape, dt=F32):
            return ctx.enter_context(nc.sbuf_tensor(name, shape, dt))

        def sem(name):
            return ctx.enter_context(nc.semaphore(name))

        ps = ctx.enter_context(nc.psum_tensor("ps", [P, 8, 512], F32))

        x = sb("x", [P, NC, D])

        def sb_rounded(name, cols):
            with nc.sbuf_tensor(name, [P, cols], F32R) as t:
                return t

        low_r = sb_rounded("low_r", 4608)
        low = sb("low", [P, 14256])
        cw_r = sb_rounded("cw_r", 4608 + 1024 * HSLOTS)
        cw = sb("cw", [P, 8192])
        big_r = sb_rounded("big_r", 1024 * WSLOTS)
        big = sb("big", [P, 4 * 6144])
        lowf = low[:, :]
        ht = lowf[:, 0:4608].rearrange("p (k t) -> p k t", k=KD)
        qk = lowf[:, 4608:9216].rearrange("p (k t) -> p k t", k=KD)
        vflat = lowf[:, 9216:11776]
        v = vflat.rearrange("p (c n) -> p c n", c=NC)
        uflat = lowf[:, 11776:14256]
        u = uflat.rearrange("p (i t) -> p i t", i=NI)

        ident = sb("ident", [P, P])
        ntri = sb("ntri", [P, P])
        nones = sb("nones", [P, P])
        identb = sb("identb", [P, P], BF16)
        negb = sb("negb", [P, P], BF16)
        tril = sb("tril", [P, P], BF16)
        onesb = sb("onesb", [P, P], BF16)
        vt = sb("vt", [P, 24])
        cwt = sb("cwt", [P, NI, TAPS])
        stat = sb("stat", [P, 48])
        stat_o = sb("stat_o", [P, NC * HEADS])
        nhalf = sb("nhalf", [P, 1])
        valid = sb("valid", [P, NC])
        bias36 = sb("bias36", [P, NG + NE])

        mixt = ht
        qt = qk[:, 0:NI, :]
        kt = qk[:, NI:2 * NI, :]
        h2t = qk
        ckt = cw[:, 0:4096].rearrange("p (i s) -> p i s", i=NI)
        cv = cw[:, 4096:8192].rearrange("p (b c) -> p b c", b=8)
        wout = cw[:, :].rearrange("p (k n) -> p k n", k=8)

        def part(lo, n):
            return big[:, lo:lo + n]

        win = [part(s * 1024, 1024).rearrange("p (k n) -> p k n", k=KD) for s in range(WSLOTS)]
        wv = part(6144, 4096).rearrange("p (k n) -> p k n", k=KD)
        ckraw = part(10240, 4096).rearrange("p (b c) -> p b c", b=8)
        conv = part(14336, 4 * (UW - HIST)).rearrange("p (i t) -> p i t", i=NI)
        yc = part(16704, NI * COLS).rearrange("p (i t) -> p i t", i=NI)
        ot = part(19008, NC * CC).rearrange("p (c n) -> p c n", c=NC)
        ht_hi = cw_r[:, 0:4608].rearrange("p (k t) -> p k t", k=KD)
        w_hi = [cw_r[:, 4608 + 1024 * s:5632 + 1024 * s].rearrange("p (k n) -> p k n", k=KD) for s in range(HSLOTS)]
        ht_lo = low_r[:, :].rearrange("p (k t) -> p k t", k=KD)
        w_lo = [big_r[:, 1024 * s:1024 * s + 1024].rearrange("p (k n) -> p k n", k=KD) for s in range(WSLOTS)]
        h1 = [part(21568 + 1024 * b, 1024) for b in range(2)]
        qpair = part(21568, 2 * NI * 64).rearrange("p (a i t) -> p a i t", a=2, i=NI)
        sgm = part(23616, COLS)
        vecrow = part(24192, P)
        lnsq = part(0, NI * COLS).rearrange("p (i t) -> p i t", i=NI)
        lnv = part(12288, COLS)
        lnt = part(12864, COLS)
        lnr = part(13440, COLS)
        convrow = part(10240, CC)
        histrow = part(10752, CC)
        sq1 = part(14336, D)
        za = [part(3072 + 512 * b, 512) for b in range(3)]
        el = [part(4608 + 512 * b, 512) for b in range(3)]
        wt = [part(6144 + 512 * b, 512) for b in range(3)]
        cs = [part(7680 + 512 * b, 512) for b in range(2)]
        cs_few = [part(2304 + 256 * b, 256) for b in range(2)]
        ko = [part(8704 + 512 * b, 512) for b in range(2)]
        co = [part(9728, 512), part(10240, 512)]
        osq = part(10752, NC * CC).rearrange("p (c n) -> p c n", c=NC)
        h2 = [vflat[:, 0:1024], uflat[:, 0:1024]]
        gff = uflat[:, 1024:2048]
        sq2 = vflat[:, 1024:2048]
        wrt = vflat[:, 2048:2048 + KD * (NG + NE)].rearrange("p (k n) -> p k n", k=KD)
        slots = [part(6144 * q, 6144) for q in range(4)] + [lowf[:, 6144 * q:6144 * q + 6144] for q in range(2)]
        wi = [t[:, 0:4096].rearrange("p (k n) -> p k n", k=KD) for t in slots]
        wo = [t[:, 4096:6144].rearrange("p (k n) -> p k n", k=2) for t in slots]
        xg = [cw[:, 1024 * b:1024 * b + 1024] for b in range(3)]
        yg = [cw[:, 3072 + 1024 * b:4096 + 1024 * b] for b in range(3)]
        rest = lowf[:, 12288:14256]
        xt = [t.rearrange("p (k t) -> p k t", k=KD) for t in (cw[:, 6144:7168], cw[:, 7168:8192], rest[:, 0:1024])]
        sil = [rest[:, 1024 + 128 * b:1152 + 128 * b].rearrange("p (k t) -> p k t", k=2) for b in range(2)]
        act2 = [rest[:, 1280 + 128 * b:1408 + 128 * b].rearrange("p (k t) -> p k t", k=2) for b in range(2)]
        tab = rest[:, 1536:1536 + 4 * PAIRS].rearrange("p (g f) -> p g f", f=4)
        idx = [rest[:, 1600 + b:1601 + b].bitcast(I32) for b in range(3)]
        oidx = [rest[:, 1604 + b:1605 + b].bitcast(I32) for b in range(3)]
        gat = [rest[:, 1608 + b:1609 + b] for b in range(3)]
        more_tab = rest[0:TILE, 1612:1616]
        fill = cw[:, 0:576]

        def rt(lo, n):
            return cw[:, 3072 + lo:3072 + lo + n]

        lg = rt(0, NC * 36).rearrange("p (c n) -> p c n", c=NC)
        lm = rt(256, NC * NE)
        eqm = rt(512, NC * NE)
        o1 = rt(768, NC * NE)
        o2 = rt(1024, NC * NE)
        tmp = rt(1280, NC * NE)
        ex = rt(1536, NC * NE)
        io32 = rt(1792, NE)
        io4 = rt(1824, NG)
        colid = rt(1832, NC)
        gex = rt(1880, NC * NG)
        og = rt(1904, NC * NG)
        ent = [rest[:, 1616 + 20 * b:1636 + 20 * b].rearrange("p (c f) -> p c f", f=4) for b in range(2)]
        adr = [rest[:, 1656 + 8 * b:1656 + 8 * b + NC].bitcast(I32) for b in range(2)]
        place = [rt(2240 + NC * TILE * b, NC * TILE).rearrange("p (c t) -> p c t", c=NC) for b in range(2)]
        entry = [rt(2880 + NC * NE * 3 * b, NC * NE * 3).rearrange("p (c e f) -> p c e f", c=NC, f=3) for b in range(2)]
        iotile = rt(3840, TILE)
        mb = rt(2000, 80).bitcast(BF16)
        sm = rt(2080, 128)
        ecol = rt(2208, NE)
        cnt = sb("cnt", [1, NE + 1], I32)
        y0 = [part(1024 * c, 1024) for c in range(NC)]
        y1 = [part(5120 + 1024 * c, 1024) for c in range(NC)]
        yo = [part(10240 + 1024 * c, 1024) for c in range(NC)]
        gfn = part(15360, 1024)
        sq3 = part(16384, 1024)

        h2_dram = nc.dram_tensor("h2_dram", (COLS, D), F32, kind="Internal").ap()
        tab_dram = nc.dram_tensor("tab_dram", (COLS * NE, 4), F32, kind="Internal").ap()
        y_dram = nc.dram_tensor("y_dram", (2 * COLS, D), F32, kind="Internal").ap()

        x_loaded = [sem(f"x_loaded{c}") for c in range(NC)]
        vec_loaded = sem("vec_loaded")
        convw_loaded = sem("convw_loaded")
        hist_loaded = sem("hist_loaded")
        win_loaded = [sem(f"win_loaded{s}") for s in range(WSLOTS)]
        wv_loaded = [sem(f"wv_loaded{q}") for q in range(4)]
        ck_loaded = sem("ck_loaded")
        cv_loaded = sem("cv_loaded")
        wout_loaded = sem("wout_loaded")
        router_loaded = sem("router_loaded")
        wi_loaded = [sem(f"wi_loaded{q}") for q in range(2 * RING)]
        wo_loaded = [sem(f"wo_loaded{q}") for q in range(2 * RING)]
        const_ready = sem("const_ready")
        pool_chain = sem("pool_chain")
        dve_chain = sem("dve_chain")
        var_ready = sem("var_ready")
        rstd_ready = sem("rstd_ready")
        ssq_ready = sem("ssq_ready")
        h_ready = sem("h_ready")
        h_turned = sem("h_turned")
        ht_ready = sem("ht_ready")
        small_turned = sem("small_turned")
        small_ready = sem("small_ready")
        ht_hi_ready = sem("ht_hi_ready")
        ht_lo_ready = sem("ht_lo_ready")
        w_hi_ready = sem("w_hi_ready")
        w_lo_ready = sem("w_lo_ready")
        proj_done = sem("proj_done")
        sig_done = sem("sig_done")
        u_done = sem("u_done")
        qk_done = sem("qk_done")
        conv_done = sem("conv_done")
        yc_ready = sem("yc_ready")
        mean_done = sem("mean_done")
        dev_ready = sem("dev_ready")
        ln_summed = sem("ln_summed")
        devsq_ready = sem("devsq_ready")
        var_done = sem("var_done")
        norm_ready = sem("norm_ready")
        ck_turned = sem("ck_turned")
        ckt_ready = sem("ckt_ready")
        v_done = sem("v_done")
        v_ready = sem("v_ready")
        qpair_ready = sem("qpair_ready")
        z_ready = sem("z_ready")
        zc_ready = sem("zc_ready")
        e_done = sem("e_done")
        l_done = sem("l_done")
        el_ready = sem("el_ready")
        cs_ready = sem("cs_ready")
        zr_ready = sem("zr_ready")
        w_ready = sem("w_ready")
        av_done = sem("av_done")
        o_ready = sem("o_ready")
        onorm_ready = sem("onorm_ready")
        o_turned = sem("o_turned")
        mixa_ready = sem("mixa_ready")
        mixb_ready = sem("mixb_ready")
        ko_turned = sem("ko_turned")
        ko_ready = sem("ko_ready")
        ko_stored = [sem(f"ko_stored{b}") for b in range(2)]
        co_turned = sem("co_turned")
        co_ready = sem("co_ready")
        small_stored = sem("small_stored")
        res_done = sem("res_done")
        x2_ready = sem("x2_ready")
        ssq2_ready = sem("ssq2_ready")
        h2_ready = sem("h2_ready")
        h2_turned = sem("h2_turned")
        h2t_ready = sem("h2t_ready")
        logit_done = sem("logit_done")
        h2_stored = [sem(f"h2_stored{b}") for b in range(2)]
        gsub_ready = sem("gsub_ready")
        gexp_ready = sem("gexp_ready")
        esub_ready = sem("esub_ready")
        eexp_ready = sem("eexp_ready")
        picks_ready = sem("picks_ready")
        pos_done = sem("pos_done")
        places_ready = sem("places_ready")
        entries_ready = sem("entries_ready")
        tab_summed = sem("tab_summed")
        tab_ready = sem("tab_ready")
        ent_ready = sem("ent_ready")
        tab_filled = sem("tab_filled")
        tab_stored = sem("tab_stored")
        zero_ready = sem("zero_ready")
        pe_passed = sem("pe_passed")
        pool_passed = sem("pool_passed")
        idx_ready = sem("idx_ready")
        gat_ready = sem("gat_ready")
        oidx_ready = sem("oidx_ready")
        gathered = [sem(f"gathered{b}") for b in range(3)]
        xg_turned = sem("xg_turned")
        xt_ready = sem("xt_ready")
        gu_done = sem("gu_done")
        sil_ready = sem("sil_ready")
        act_ready = sem("act_ready")
        y_done = sem("y_done")
        yg_ready = sem("yg_ready")
        scattered = [sem(f"scattered{b}") for b in range(3)]
        more_free = sem("more_free")
        more_loaded = sem("more_loaded")
        more_idx = sem("more_idx")
        more_gathered = sem("more_gathered")
        more_turned = sem("more_turned")
        more_xt = sem("more_xt")
        more_gu = sem("more_gu")
        more_sil = sem("more_sil")
        more_act = sem("more_act")
        more_rows = sem("more_rows")
        more_scaled = sem("more_scaled")
        more_scattered = sem("more_scattered")
        experts_done = sem("experts_done")
        y_loaded = [sem(f"y_loaded{c}") for c in range(NC)]
        gfn_loaded = sem("gfn_loaded")
        sum_ready = sem("sum_ready")
        ssq3_ready = sem("ssq3_ready")
        yo_ready = sem("yo_ready")
        yo2_ready = sem("yo2_ready")
        scaled = sem("scaled")
        yo_stored = sem("yo_stored")
        y01_ready = sem("y01_ready")
        lnl_done = sem("lnl_done")
        lnr_done = sem("lnr_done")
        lnv_ready = sem("lnv_ready")

        ROOTS_BEFORE = NC + 2 + NC
        N_CONST = 18

        few, many = [], []
        for unit, (q0, p0, blocks) in enumerate([(S0, 32, 9), (512, 0, 5)]):
            for n in range(blocks):
                own = n == 0
                b = blocks - 1 - n
                st = dict(unit=unit, n=HEADS * 32, first=own, last=n == blocks - 1,
                          rows=(p0, p0 + 32) if own else (0, P), q0=q0, p0=p0, b=b, own=own)
                few.append(st)
        for h in range(HEADS):
            for b in range(3, -1, -1):
                many.append(dict(unit=2 + h, h=h, b=b, n=512 - P * b, first=b == 3, last=b == 0,
                                 rows=(0, P)))
        for lst, bufs in ((few, cs_few), (many, cs)):
            for j, st in enumerate(lst):
                st.update(cs=bufs[j % 2], old=bufs[(j - 1) % 2], before=lst[j - 1] if j else None)
        steps, a, b = [], list(few), list(many)
        while a or b:
            steps += [a.pop(0) for _ in range(min(2, len(a)))]
            if b:
                steps.append(b.pop(0))
        NS = len(steps)
        for s, st in enumerate(steps):
            st["s"] = s
        ended = {}
        for st in steps:
            if st["last"]:
                ended[st["unit"]] = len(ended) + 1
        sums = [sum(not st["last"] for st in steps[:s + 1]) for s in range(NS)]
        unit_bank = lambda unit: 6 + unit if unit < 2 else 4 + unit % 2

        block = ctx.enter_context(nc.Block())

        def pair_loop(eng, step, tail=0):
            for g in range(RING):
                step(g, g, 0)
            rounds = (PAIRS - tail) // RING
            with eng.Fori(1, rounds) as n:
                for s in range(RING):
                    step(n * RING + s, s, n)
            for g in range(rounds * RING, PAIRS):
                step(g, g % RING, g // RING)

        def peeled(g):
            return isinstance(g, int)

        def each_further_tile(eng, tile, before=lambda: None):
            eng.wait_ge(ent_ready, 1)
            most = eng.value_load(cnt[0:1, NE:NE + 1], min_val=0, max_val=COLS)
            with eng.If(most > TILE):
                before()
                n = eng.alloc_register("tiles")
                eng.reg_mov(n, 0)
                with eng.Fori(0, NE) as e:
                    tokens = eng.value_load(cnt[0:1, bass.ds(e, 1)], min_val=0, max_val=COLS)
                    with eng.If(tokens > TILE):
                        tiles = eng.snap((tokens + (TILE - 1)) // TILE, min_val=2, max_val=NTILE)
                        with eng.Fori(1, tiles) as t:
                            tile(eng.snap(n, min_val=0, max_val=2 * NTILE), e, t)
                            eng.reg_add(n, n, 1)

        @block.sync
        def _(sp):
            xp = x_prompt[0]
            sp.dma_start(x[0:META, 0, :], meta).then_inc(x_loaded[0], 16)
            sp.dma_start(x[META:P, 0, :], xp[0:P - META]).then_inc(x_loaded[0], 16)
            for r, g in enumerate((g_mix, conv_b, ln_g, ln_b, g_sb)):
                lo = 0 if r == 0 else 8 + 4 * (r - 1)
                k = 8 if r == 0 else 4
                sp.dma_start(vecrow[lo:lo + k, :], g[0].rearrange("(k n) -> k n", k=k)).then_inc(vec_loaded, 16)
            w3 = w_in[0].rearrange("(k p) n -> p k n", p=P)

            def load_x(c):
                lo = P * c - META
                sp.dma_start(x[:, c, :], xp[lo:lo + P]).then_inc(x_loaded[c], 16)

            for part4 in range(4):
                sp.dma_start(wv[:, 2 * part4:2 * part4 + 2, :], w3[:, 2 * part4:2 * part4 + 2, 4 * CC:5 * CC]).then_inc(wv_loaded[part4], 16)
                if part4 == 1:
                    load_x(1)
            load_x(2)
            load_x(3)
            sp.wait_ge(const_ready, 1)
            sp.dma_start(x[0:META, 4, :], xp[SEQ - META:SEQ]).then_inc(x_loaded[4], 16)
            sp.dma_start(x[32:64, 4, :], x_sample[0]).then_inc(x_loaded[4], 16)
            sp.dma_start(convrow[0:TAPS, :], conv_w[0]).then_inc(convw_loaded, 16)
            sp.dma_start(histrow[0:HIST, :], cache_conv[0, 0]).then_inc(hist_loaded, 16)
            starts = []
            for i in range(NI):
                starts += [CC + P * i, P * i]
            for i in range(NI):
                starts += [3 * CC + P * i, 2 * CC + P * i]
            for j, lo in enumerate(starts):
                if j >= WSLOTS:
                    sp.wait_ge(proj_done, j - WSLOTS + 1)
                sp.dma_start(win[j % WSLOTS], w3[:, :, lo:lo + P]).then_inc(win_loaded[j % WSLOTS], 16)
                if j == WSLOTS:
                    sp.wait_ge(small_ready, 3)
                    sp.dma_start(ckraw, cache_k[0, 0].rearrange("(b p) h d -> p b (h d)", p=P)).then_inc(ck_loaded, 16)
            sp.wait_ge(proj_done, 16)
            sp.dma_start(cv, cache_v[0, 0].rearrange("(b p) h d -> p b (h d)", p=P)).then_inc(cv_loaded, 16)
            for c in range(4):
                sp.wait_ge(v_ready, c + 1)
                sp.dma_start(nv_p[0, 0, P * c:P * c + P].rearrange("t h d -> t (h d)"), v[:, c, :]).then_inc(small_stored, 16)
            sp.wait_ge(v_ready, 5)
            sp.dma_start(nv_p[0, 0, 512:TP].rearrange("t h d -> t (h d)"), v[0:16, 4, :]).then_inc(small_stored, 16)
            sp.dma_start(nv_s[0, 0].rearrange("t h d -> t (h d)"), v[32:64, 4, :]).then_inc(small_stored, 16)
            sp.wait_ge(av_done, few[8]["s"] + 1)
            sp.dma_start(wout, w_out[0].rearrange("(k p) n -> p k n", p=P)).then_inc(wout_loaded, 16)
            for c in range(NC):
                sp.wait_ge(ko_ready, c + 1)
                src = ko[c % 2]
                if c < 4:
                    sp.dma_start(nk_p[0, 0, P * c:P * c + P].rearrange("t h d -> t (h d)"), src).then_inc(ko_stored[c % 2], 16)
                else:
                    sp.dma_start(nk_p[0, 0, 512:TP].rearrange("t h d -> t (h d)"), src[0:16, :]).then_inc(ko_stored[c % 2], 16)
                    sp.dma_start(nk_s[0, 0].rearrange("t h d -> t (h d)"), src[32:64, :]).then_inc(ko_stored[c % 2], 16)
            sp.wait_ge(co_ready, 2)
            sp.dma_start(ncv_p[0, 0], co[0][0:HIST, :]).then_inc(small_stored, 16)
            sp.dma_start(ncv_s[0, 0], co[1][0:HIST, :]).then_inc(small_stored, 16)
            sp.wait_ge(mixa_ready, NI)
            sp.wait_ge(mixb_ready, NC)
            sp.wait_ge(ko_stored[0], 16 * 4)
            sp.wait_ge(ko_stored[1], 16 * 2)
            sp.wait_ge(small_stored, 16 * 8)
            sp.dma_start(wrt[:, :, 0:NG], w_rg[0].rearrange("(k p) n -> p k n", p=P)).then_inc(router_loaded, 16)
            sp.dma_start(wrt[:, :, NG:], w_re[0].rearrange("(k p) n -> p k n", p=P)).then_inc(router_loaded, 16)
            sp.dma_start(gff, g_ffn[0:1].broadcast_to([P, D])).then_inc(router_loaded, 16)
            sp.dma_start(bias36[:, 0:NG], b_rg[0:1].broadcast_to([P, NG])).then_inc(router_loaded, 16)
            sp.dma_start(bias36[:, NG:], b_re[0:1].broadcast_to([P, NE])).then_inc(router_loaded, 16)

            def load_wi(g, s, half):
                q = 2 * s + half
                if not peeled(g) or g >= RING:
                    sp.wait_ge(gu_done, (g - RING) * 2 + half + 1)
                e = bass.ds(g * 2 + half, 1)
                sp.dma_start(wi[q], w_ei[0, e].rearrange("a (k p) n -> p (a k) n", p=P)).then_inc(wi_loaded[q], 16)

            def load_wo(g, s):
                if not peeled(g) or g >= RING:
                    sp.wait_ge(y_done, g - RING + 1)
                for half in range(2):
                    q = 2 * s + half
                    e = bass.ds(g * 2 + half, 1)
                    sp.dma_start(wo[q], w_eo[0, e].rearrange("a (k p) n -> p (a k) n", p=P)).then_inc(wo_loaded[q], 16)

            load_wi(0, 0, 0)
            load_wi(0, 0, 1)
            for c in range(NC):
                sp.wait_ge(h2_ready, c + 1)
                sp.dma_start(h2_dram[P * c:P * c + ROWS[c], :], h2[c % 2][0:ROWS[c], :]).then_inc(h2_stored[c % 2], 16)
                if c == 0:
                    load_wo(0, 0)
                elif c < 3:
                    load_wi(1, 1, c - 1)
                elif c == 3:
                    load_wo(1, 1)
            sp.wait_ge(logit_done, NC)
            sp.wait_ge(h2_stored[0], 16 * 3)
            sp.wait_ge(h2_stored[1], 16 * 2)
            load_wi(2, 2, 0)
            load_wi(2, 2, 1)
            sp.wait_ge(gathered[1], 16)
            load_wo(2, 2)

            def step(g, s):
                load_wi(g, s, 0)
                if not (peeled(g) and g == RING):
                    load_wo(g - 1, (s - 1) % RING)
                load_wi(g, s, 1)

            for g in range(RING, 2 * RING):
                step(g, g % RING)
            with sp.Fori(2, PAIRS // RING) as n:
                for s in range(RING):
                    step(n * RING + s, s)
            for g in range(PAIRS // RING * RING, PAIRS):
                step(g, g % RING)
            load_wo(PAIRS - 1, (PAIRS - 1) % RING)

            sp.wait_ge(y_done, PAIRS - 2)
            sp.dma_start(gfn, g_fin.rearrange("(a d) -> a d", a=1).broadcast_to([P, D])).then_inc(gfn_loaded, 16)

            def more(n, e, t):
                sp.wait_ge(more_free, n + 1)
                sp.dma_start(more_tab, tab_dram[bass.ds(t * (TILE * NE), TILE * NE), :].rearrange(
                    "(s m) f -> s m f", m=NE)[:, bass.ds((e % 2) * PAIRS + e // 2, 1), :].rearrange(
                    "s m f -> s (m f)")).then_inc(more_loaded, 16)
                sp.dma_start(wi[0], w_ei[0, bass.ds(e, 1)].rearrange("a (k p) n -> p (a k) n", p=P)).then_inc(more_loaded, 16)
                sp.dma_start(wo[0], w_eo[0, bass.ds(e, 1)].rearrange("a (k p) n -> p (a k) n", p=P)).then_inc(more_loaded, 16)

            each_further_tile(sp, more)
            sp.wait_ge(experts_done, 1)
            for c in range(NC):
                for k, dst in enumerate((y0[c], y1[c])):
                    lo = k * COLS + P * c
                    if c < 4:
                        sp.dma_start(dst, y_dram[lo:lo + P, :]).then_inc(y_loaded[c], 16)
                    else:
                        sp.dma_start(dst[0:16, :], y_dram[lo:lo + 16, :]).then_inc(y_loaded[c], 16)
                        sp.dma_start(dst[32:64, :], y_dram[lo + 32:lo + 64, :]).then_inc(y_loaded[c], 16)
            for c in range(NC):
                if c in POOL_NORMS:
                    sp.wait_ge(yo2_ready, POOL_NORMS.index(c) + 1)
                else:
                    sp.wait_ge(yo_ready, c + 1 - sum(q < c for q in POOL_NORMS))
                if c == 0:
                    sp.dma_start(y_p[0, 0:P - META], yo[c][META:P, :]).then_inc(yo_stored, 16)
                elif c < 4:
                    sp.dma_start(y_p[0, P * c - META:P * c + P - META], yo[c]).then_inc(yo_stored, 16)
                else:
                    sp.dma_start(y_p[0, SEQ - META:SEQ], yo[c][0:16, :]).then_inc(yo_stored, 16)
                    sp.dma_start(y_s[0], yo[c][32:64, :]).then_inc(yo_stored, 16)
            sp.wait_ge(yo_stored, 16 * 6)

        @block.gpsimd
        def _(pool):
            done = [0]

            def const(ins):
                done[0] += 1
                ins.then_inc(const_ready, 1)

            def settled():
                pool.wait_ge(const_ready, done[0])

            const(pool.memset(x[0:64, 4, :], 0.0))
            const(pool.memset(nhalf[:, :], -0.5))
            const(pool.memset(ident[:, :], 1.0))
            const(pool.memset(ntri[:, :], -1.0))
            const(pool.memset(nones[:, :], -1.0))
            const(pool.memset(identb[:, :], 1.0))
            const(pool.memset(negb[:, :], NEG))
            const(pool.memset(tril[:, :], 1.0))
            const(pool.memset(onesb[:, :], 1.0))
            const(pool.memset(u[:, :, 0:HIST], 0.0))
            const(pool.memset(valid[:, :], 1.0))
            const(pool.memset(yc[:, :, TP:S0], 0.0))
            settled()

            def keep(t, op, mult, fill=0.0):
                const(pool.affine_select(out=t, in_=t, pattern=[[-mult, P]], compare_op=op, fill=fill,
                                         base=0, channel_multiplier=mult))
            keep(ident[:, :], ALU.is_equal, 1)
            keep(ntri[:, :], ALU.is_ge, 1)
            keep(identb[:, :], ALU.is_equal, 1)
            keep(negb[:, :], ALU.is_ge, 1)
            keep(tril[:, :], ALU.is_gt, -1)
            const(pool.memset(valid[:, 4:5], 0.0))
            assert done[0] == N_CONST

            roots = [0]

            def root(t):
                roots[0] += 1
                pool.wait_ge(var_ready, roots[0])
                pool.tensor_tensor(t, t, nhalf[0:t.shape[0], :].broadcast_to(list(t.shape)), ALU.pow).then_inc(rstd_ready, 1)

            for c in range(NC):
                root(stat[0:ROWS[c], 24 + c:25 + c])

            pool.wait_ge(h_turned, NC)
            pool.memset(qpair, 0.0).then_inc(qpair_ready, 1)
            pool.wait_ge(qpair_ready, 1)
            def lower(j):
                slot = win[j % WSLOTS]
                pool.wait_ge(w_hi_ready, j + 1)
                pool.tensor_tensor(w_lo[j % WSLOTS], slot, w_hi[j % HSLOTS].bitcast(F32), ALU.subtract).then_inc(w_lo_ready, 1)

            for j in range(13):
                lower(j)
            for i in range(NI):
                split = min(13 + 2 * i, 16)
                if i in (1, 2):
                    pool.wait_ge(qpair_ready, 2 * i + 1)
                    for j in range(11 + 2 * i, split):
                        lower(j)
                pool.wait_ge(w_lo_ready, split)
                pool.wait_ge(qk_done, 2 * i + 2)
                for r in range(2):
                    pool.tensor_copy(qpair[64 * r:64 * r + 64, :, i, 32 * r:32 * r + 32],
                                     qt[64 * r:64 * r + 64, i, 512:COLS].rearrange("p (a t) -> p a t", a=2)).then_inc(qpair_ready, 1)
            pool.wait_ge(z_ready, 1)
            for s, st in enumerate(steps):
                r0, r1 = st["rows"]
                n = st["n"]
                i = s - LN_STEP + NI
                if 1 <= i < NI:
                    pool.wait_ge(yc_ready, 2 * NI)
                    if i >= 2:
                        pool.wait_ge(ln_summed, i - 1)
                    pool.tensor_tensor(lnt, yc[:, 0, :] if i == 1 else lnt, yc[:, i, :], ALU.add).then_inc(ln_summed, 1)
                i = s - LN_STEP - 3
                if 1 <= i < NI:
                    pool.wait_ge(devsq_ready, i + 1)
                    if i >= 2:
                        pool.wait_ge(ln_summed, NI - 2 + i)
                    pool.tensor_tensor(lnr, lnsq[:, 0, :] if i == 1 else lnr, lnsq[:, i, :], ALU.add).then_inc(ln_summed, 1)
                if st["before"]:
                    pool.wait_ge(zr_ready, st["before"]["s"] + 1)
                if st["last"]:
                    continue
                new, old = st["cs"], st["old"]
                if "h" in st:
                    c0 = P * st["b"]
                    pool.wait_ge(el_ready, s + 1)
                    if st["first"]:
                        pool.tensor_copy(new[:, c0:c0 + P], el[s % 3][:, 0:P]).then_inc(cs_ready, 1)
                    else:
                        pool.wait_ge(cs_ready, sums[st["before"]["s"]])
                        pool.tensor_copy(new[:, c0:c0 + P], el[s % 3][:, 0:P])
                        pool.tensor_tensor(new[:, c0 + P:512], old[:, c0 + P:512], el[s % 3][:, P:n],
                                           ALU.add).then_inc(cs_ready, 1)
                elif st["first"]:
                    pool.memset(new[:, 0:n], 0.0).then_inc(pool_chain, 1)
                    pool.wait_ge(el_ready, s + 1)
                    pool.wait_ge(pool_chain, st["unit"] + 1)
                    pool.tensor_copy(new[r0:r1, 0:n], el[s % 3][r0:r1, 0:n]).then_inc(cs_ready, 1)
                else:
                    pool.wait_ge(el_ready, s + 1)
                    pool.wait_ge(cs_ready, sums[st["before"]["s"]])
                    pool.tensor_tensor(new[:, 0:n], old[:, 0:n], el[s % 3][:, 0:n], ALU.add).then_inc(cs_ready, 1)

            root(stat_o[:, 0:4 * HEADS])
            root(stat_o[0:64, 4 * HEADS:5 * HEADS])
            for c in range(NC):
                root(stat[0:ROWS[c], 32 + c:33 + c])

            pool.wait_ge(res_done, NC)
            pool.memset(cw[:, 0:3072], 0.0).then_inc(zero_ready, 1)
            pool.iota(io32, [[1, NE]], base=0, channel_multiplier=0, allow_small_or_imprecise_dtypes=True).then_inc(zero_ready, 1)
            pool.iota(ecol, [[1, PAIRS], [PAIRS, 2]], base=0, channel_multiplier=0, allow_small_or_imprecise_dtypes=True).then_inc(zero_ready, 1)
            pool.iota(io4, [[1, NG]], base=0, channel_multiplier=0, allow_small_or_imprecise_dtypes=True).then_inc(zero_ready, 1)
            pool.iota(iotile, [[1, TILE]], base=0, channel_multiplier=0, allow_small_or_imprecise_dtypes=True).then_inc(zero_ready, 1)
            pool.iota(colid, [[P, NC]], base=0, channel_multiplier=1, allow_small_or_imprecise_dtypes=True).then_inc(zero_ready, 1)
            pool.memset(lg[:, 4, :], 0.0).then_inc(zero_ready, 1)
            pool.memset(ent[0], 0.0).then_inc(zero_ready, 1)
            pool.memset(ent[1], 0.0).then_inc(zero_ready, 1)
            pool.wait_ge(tab_ready, 2)
            pool.wait_ge(h2_stored[0], 16 * 3)
            pool.wait_ge(h2_stored[1], 16 * 2)
            pool.wait_ge(zero_ready, 9)

            def gather(g, s):
                if not peeled(g) or g >= RING:
                    pool.wait_ge(xg_turned, g - RING + 1)
                pool.tensor_copy(idx[s], tab[:, bass.ds(g, 1), 0:1].rearrange("p a f -> p (a f)")).then_inc(idx_ready, 1)
                pool.wait_ge(idx_ready, g + 1)
                pool.sem_inc(pool_passed, 1)
                pool.indirect_dma_start(
                    out=xg[s], out_offset=None, in_=h2_dram,
                    in_offset=bass.IndirectOffsetOnAxis(ap=idx[s].bitcast(U32), axis=0),
                    bounds_check=COLS - 1, oob_is_err=False).then_inc(gathered[s], 16)

            def gates(g, s):
                if not peeled(g) or g >= RING:
                    pool.wait_ge(yg_ready, g - RING + 1)
                pool.tensor_copy(gat[s], tab[:, bass.ds(g, 1), 2:3].rearrange("p a f -> p (a f)")).then_inc(gat_ready, 1)

            def scatter(g, s, n):
                if not peeled(g) or g >= RING:
                    pool.wait_ge(scattered[s], n * 16)
                pool.tensor_copy(oidx[s], tab[:, bass.ds(g, 1), 1:2].rearrange("p a f -> p (a f)")).then_inc(oidx_ready, 1)
                pool.wait_ge(oidx_ready, g + 1)
                pool.wait_ge(yg_ready, g + 1)
                pool.sem_inc(pool_passed, 1)
                pool.indirect_dma_start(
                    out=y_dram, out_offset=bass.IndirectOffsetOnAxis(ap=oidx[s].bitcast(U32), axis=0),
                    in_=yg[s], in_offset=None, bounds_check=2 * COLS - 1,
                    oob_is_err=False).then_inc(scattered[s], 16)

            def step(g, s, n):
                gather(g, s)
                gates(g - LAG + RING, (s - LAG) % RING)
                scatter(g - LAG, (s - LAG) % RING, n - 2 if s < LAG - RING else n - 1)

            for g in range(RING):
                gather(g, g)
                gates(g, g)
            for g in range(RING, LAG):
                gather(g, g % RING)
            for g in range(LAG, 3 * RING):
                step(g, g % RING, g // RING)
            with pool.Fori(3, PAIRS // RING) as n:
                for s in range(RING):
                    step(n * RING + s, s, n)
            for g in range(PAIRS // RING * RING, PAIRS):
                step(g, g % RING, g // RING)
            for g in range(PAIRS - LAG, PAIRS):
                if g + RING < PAIRS:
                    gates(g + RING, g % RING)
                scatter(g, g % RING, g // RING)
            for b in range(3):
                pool.wait_ge(scattered[b], 16 * len(range(b, PAIRS, 3)))

            def more(n, e, t):
                pool.wait_ge(more_loaded, n * 48 + 48)
                pool.sem_inc(pool_passed, 1)
                pool.tensor_copy(idx[0][0:TILE], more_tab[:, 0:1]).then_inc(more_idx, 1)
                pool.tensor_copy(oidx[0][0:TILE], more_tab[:, 1:2]).then_inc(more_idx, 1)
                pool.wait_ge(more_idx, n * 2 + 2)
                pool.sem_inc(pool_passed, 1)
                pool.indirect_dma_start(
                    out=xg[0][0:TILE], out_offset=None, in_=h2_dram,
                    in_offset=bass.IndirectOffsetOnAxis(ap=idx[0][0:TILE].bitcast(U32), axis=0),
                    bounds_check=COLS - 1, oob_is_err=False).then_inc(more_gathered, 16)
                pool.wait_ge(more_scaled, n + 1)
                pool.sem_inc(pool_passed, 1)
                pool.indirect_dma_start(
                    out=y_dram, out_offset=bass.IndirectOffsetOnAxis(ap=oidx[0][0:TILE].bitcast(U32), axis=0),
                    in_=yg[0][0:TILE], in_offset=None, bounds_check=2 * COLS - 1,
                    oob_is_err=False).then_inc(more_scattered, 16)
                pool.wait_ge(more_scattered, n * 16 + 16)
                pool.sem_inc(more_free, 1)

            def table():
                pool.memset(fill, BIGF).then_inc(pool_chain, 1)
                pool.wait_ge(pool_chain, 3)
                pool.dma_start(tab_dram.rearrange("(p r) f -> p (r f)", p=P), fill).then_inc(tab_filled, 16)
                pool.wait_ge(tab_filled, 16)
                for k in range(2):
                    for c in range(NC):
                        w = ROWS[c]
                        pool.indirect_dma_start(
                            out=tab_dram, out_offset=bass.IndirectOffsetOnAxis(ap=adr[k][0:w, c:c + 1].bitcast(U32), axis=0),
                            in_=ent[k][0:w, c, :], in_offset=None, bounds_check=COLS * NE - 1,
                            oob_is_err=False).then_inc(tab_stored, 16)
                pool.wait_ge(tab_stored, 16 * 2 * NC)
                pool.sem_inc(more_free, 1)

            each_further_tile(pool, more, table)
            pool.sem_inc(experts_done, 1)
            def scale_out(c):
                pool.wait_ge(scaled, POOL_NORMS.index(c) + 1)
                pool.wait_ge(gfn_loaded, 16)
                pool.tensor_tensor(yo[c], yo[c], gfn, ALU.mult).then_inc(yo2_ready, 1)

            for c in range(NC):
                w = ROWS[c]
                if c in POOL_ADDS:
                    pool.wait_ge(y_loaded[c], 32)
                    pool.tensor_tensor(y0[c][0:w, :], y0[c][0:w, :], y1[c][0:w, :], ALU.add).then_inc(y01_ready, 1)
                if c >= 1:
                    root(stat[0:ROWS[c - 1], 39 + c:40 + c])
                if c - 2 in POOL_NORMS:
                    scale_out(c - 2)
            root(stat[0:ROWS[4], 44:45])

        @block.tensor
        def _(pe):
            pe.wait_ge(const_ready, N_CONST)
            pe.wait_ge(vec_loaded, 16 * 5)
            pe.transpose(ps[:, 7, 0:24], vecrow[0:24, :], ident[0:24, 0:24]).then_inc(small_turned, 1)
            def turn_input(c):
                w = ROWS[c]
                pe.wait_ge(h_ready, c + 1)
                if c >= 2:
                    pe.wait_ge(ht_ready, c - 1)
                pt = ps[:, 2 * (c % 2):2 * (c % 2) + 2, :].rearrange("p b (k t) -> p (b k) t", t=P)
                for k in range(KD):
                    mm = pe.transpose(pt[:, k, 0:w], h1[c % 2][0:w, P * k:P * k + P], ident[0:w, 0:w])
                mm.then_inc(h_turned, 1)

            def values(c):
                if c >= 2:
                    pe.wait_ge(v_ready, c - 1)
                w = ROWS[c]
                pe.wait_ge(ht_ready, c + 1)
                for k in range(KD):
                    if c == 0 and k % 2 == 0:
                        pe.wait_ge(wv_loaded[k // 2], 16)
                    mm = pe.matmul(ps[0:w, 4 + c % 2, :], ht[:, k, P * c:P * c + w], wv[:, k, :],
                                   start=k == 0, stop=k == KD - 1)
                mm.then_inc(v_done, 1)

            turn_input(0)
            turn_input(1)
            for c in range(2, NC):
                values(c - 2)
                turn_input(c)
            pe.wait_ge(small_ready, 1)
            pe.wait_ge(convw_loaded, 16)
            for i in range(NI):
                mm = pe.transpose(ps[:, 7, 31 * i:31 * i + 31], convrow[0:TAPS, P * i:P * i + P], ident[0:TAPS, 0:TAPS])
            mm.then_inc(small_turned, 1)
            pe.wait_ge(hist_loaded, 16)
            for i in range(NI):
                mm = pe.transpose(ps[:, 6, 30 * i:30 * i + 30], histrow[0:HIST, P * i:P * i + P], ident[0:HIST, 0:HIST])
            mm.then_inc(small_turned, 1)
            values(3)
            values(4)
            pe.wait_ge(ht_hi_ready, NC)
            pe.wait_ge(ht_lo_ready, NC)
            for j in range(16):
                pe.wait_ge(w_hi_ready, j + 1)
                pe.wait_ge(w_lo_ready, j + 1)
                if 2 <= j < 10 and j % 2 == 0:
                    pe.wait_ge(sig_done, (j - 2) // 2 + 1)
                elif 2 <= j < 10:
                    pe.wait_ge(u_done, (j - 3) // 2 + 1)
                elif j >= 10:
                    pe.wait_ge(qk_done, j - 9)
                for half in range(2):
                    cols = slice(HALF * half, HALF * half + HALF)
                    for k in range(KD):
                        for m, (w, h) in enumerate(((w_hi[j % HSLOTS], ht_hi), (w_hi[j % HSLOTS], ht_lo), (w_lo[j % WSLOTS], ht_hi))):
                            mm = pe.matmul(ps[:, 2 * (j % 2) + half, 0:HALF], w[:, k, :],
                                           h[:, k, cols], start=k == 0 and m == 0,
                                           stop=k == KD - 1 and m == 2)
                mm.then_inc(proj_done, 1)
            pe.wait_ge(ck_loaded, 16)
            for b in range(8):
                if b >= 2:
                    pe.wait_ge(ckt_ready, b - 1)
                elif b == 0:
                    pe.wait_ge(small_ready, 3)
                for i in range(NI):
                    mm = pe.transpose(ps[:, 6 + b % 2, P * i:P * i + P], ckraw[:, b, P * i:P * i + P], ident[:, :])
                mm.then_inc(ck_turned, 1)
            pe.wait_ge(qk_done, 8)
            def scores(s):
                st, z = steps[s], ps[:, s % 4, :]
                if s >= 4:
                    pe.wait_ge(w_ready, s - 3)
                if "h" in st:
                    i, r, b = st["h"] // 2, 64 * (st["h"] % 2), st["b"]
                    pe.matmul(z[:, 0:st["n"]], kt[r:r + 64, i, P * b:P * b + P], qt[r:r + 64, i, P * b:512],
                              start=True, stop=True)
                    pe.matmul(z[:, 0:P], identb[:, :], negb[:, :], start=False, stop=True,
                              skip_group_check=True).then_inc(z_ready, 1)
                    return
                q0, n, (r0, r1) = st["q0"], st["n"], st["rows"]
                for i in range(NI):
                    if st["own"]:
                        keys = kt[:, i, q0:q0 + 32]
                    elif st["unit"] == 0:
                        keys = ckt[:, i, P * st["b"]:P * st["b"] + P]
                    else:
                        keys = kt[:, i, P * st["b"]:P * st["b"] + P]
                    mm = pe.matmul(z[r0:r1, 64 * i:64 * i + 64], keys, qpair[:, 1 - st["unit"], i, :],
                                   start=i == 0, stop=True, skip_group_check=True)
                if st["own"]:
                    mm = pe.matmul(z[r0:r1, 0:n], identb[r0:r1, r0:r1],
                                   negb[r0:r1, r0:r1].unsqueeze(1).broadcast_to([r1 - r0, HEADS, 32]),
                                   start=False, stop=True, skip_group_check=True)
                mm.then_inc(z_ready, 1)

            def reduce_later(s):
                st, z = steps[s], ps[:, s % 4, :]
                (r0, r1), n = st["rows"], st["n"]
                pe.wait_ge(el_ready, s + 1)
                if not st["first"]:
                    pe.wait_ge(cs_ready, sums[st["before"]["s"]])
                    old = st["old"]
                    if "h" in st:
                        pe.matmul(z[:, P:n], nones[:, :], old[:, P * st["b"] + P:512], start=False, stop=True,
                                  skip_group_check=True)
                    else:
                        pe.matmul(z[:, 0:n], nones[:, :], old[:, 0:n], start=False, stop=True,
                                  skip_group_check=True)
                pe.matmul(z[r0:r1, 0:n], ntri[r0:r1, r0:r1], el[s % 3][r0:r1, 0:n], start=False, stop=True,
                          skip_group_check=True).then_inc(zr_ready, 1)

            def weigh(s):
                st = steps[s]
                w, o = wt[s % 3], ps[:, unit_bank(st["unit"]), :]
                (r0, r1), b = st["rows"], st["b"]
                if st["unit"] >= 4 and st["first"]:
                    pe.wait_ge(o_ready, ended[st["unit"] - 2])
                pe.wait_ge(w_ready, s + 1)
                if "h" in st:
                    h = st["h"]
                    for t in range(3, b - 1, -1):
                        mm = pe.matmul(o[:, 64 * t:64 * t + 64], w[:, P * (t - b):P * (t - b) + P],
                                       v[:, b, 64 * h:64 * h + 64], start=st["first"] and t == 3, stop=True,
                                       skip_group_check=True)
                else:
                    p0 = st["p0"]
                    for h in range(HEADS):
                        if st["own"]:
                            vals = v[r0:r1, 4, 64 * h:64 * h + 64]
                        elif st["unit"] == 0:
                            if h == 0 and b == 7:
                                pe.wait_ge(cv_loaded, 16)
                            vals = cv[:, b, 64 * h:64 * h + 64]
                        else:
                            vals = v[:, b, 64 * h:64 * h + 64]
                        mm = pe.matmul(o[p0:p0 + 32, 64 * h:64 * h + 64], w[r0:r1, 32 * h:32 * h + 32], vals,
                                       start=st["first"] and h == 0, stop=True, skip_group_check=True)
                mm.then_inc(av_done, 1)

            def mean():
                pe.wait_ge(o_ready, max(ended[0], ended[1]))
                pe.wait_ge(ln_summed, NI - 1)
                for half in range(2):
                    mm = pe.matmul(ps[:, 6 + half, 0:HALF], nones[:, :], lnt[:, HALF * half:HALF * half + HALF],
                                   start=True, stop=True)
                mm.then_inc(mean_done, 1)

            def variance():
                pe.wait_ge(ln_summed, 2 * (NI - 1))
                for half in range(2):
                    mm = pe.matmul(ps[:, 6 + half, 0:HALF], nones[:, :], lnr[:, HALF * half:HALF * half + HALF],
                                   start=True, stop=True)
                mm.then_inc(var_done, 1)

            pe.wait_ge(ckt_ready, 8)
            pe.wait_ge(v_ready, NC)
            pe.wait_ge(qpair_ready, 1 + 2 * NI)
            for s in range(NS + 3):
                if s < NS:
                    scores(s)
                if s == LN_STEP:
                    mean()
                if s == LN_STEP + 9:
                    variance()
                if 2 <= s < NS + 2:
                    reduce_later(s - 2)
                if s >= 3:
                    weigh(s - 3)

            pe.wait_ge(lnv_ready, 1)
            for c in range(NC):
                if c >= 2:
                    pe.wait_ge(ko_ready, c - 1)
                w = ROWS[c]
                for i in range(NI):
                    mm = pe.transpose(ps[0:w, 6 + c % 2, P * i:P * i + P], kt[:, i, P * c:P * c + w], ident[:, :])
                mm.then_inc(ko_turned, 1)
            pe.wait_ge(w_ready, NS)
            for b, lo in enumerate((US - HIST, US + TS)):
                for i in range(NI):
                    mm = pe.transpose(ps[0:HIST, b, P * i:P * i + P], u[:, i, lo:lo + HIST], ident[:, :])
                mm.then_inc(co_turned, 1)
            pe.wait_ge(mixa_ready, NI)
            pe.wait_ge(wout_loaded, 16)
            pe.wait_ge(ko_ready, NC)
            pe.wait_ge(o_ready, 2 + HEADS)

            def project(c, ks):
                w = ROWS[c]
                for n in range(2):
                    for k in ks:
                        mm = pe.matmul(ps[0:w, 4 + 2 * (c % 2) + n, :], mixt[:, k, P * c:P * c + w],
                                       wout[:, k, 512 * n:512 * n + 512], start=k == 0, stop=k == KD - 1,
                                       skip_group_check=True)
                if ks.stop == KD:
                    mm.then_inc(res_done, 1)

            project(0, range(NI))
            project(1, range(NI))
            for c in range(NC):
                w = ROWS[c]
                if c == 0:
                    pe.wait_ge(onorm_ready, 1)
                elif c >= 2:
                    pe.wait_ge(mixb_ready, c - 1)
                for i in range(NI):
                    mm = pe.transpose(ps[:, 2 + c % 2, P * i:P * i + w], ot[0:w, c, P * i:P * i + P], ident[0:w, 0:w])
                mm.then_inc(o_turned, 1)
            pe.wait_ge(mixb_ready, NC)

            def turn_h2(c):
                w = ROWS[c]
                pe.wait_ge(h2_ready, c + 1)
                if c >= 1:
                    pe.wait_ge(h2t_ready, c)
                else:
                    pe.wait_ge(co_ready, 2)
                pt = ps[:, 0:2, :].rearrange("p b (k t) -> p (b k) t", t=P)
                for k in range(KD):
                    mm = pe.transpose(pt[:, k, 0:w], h2[c % 2][0:w, P * k:P * k + P], ident[0:w, 0:w])
                mm.then_inc(h2_turned, 1)

            def logits(c):
                if c == 0:
                    pe.wait_ge(router_loaded, 16 * 5)
                    pe.wait_ge(mixb_ready, NC)
                w = ROWS[c]
                pe.wait_ge(h2t_ready, c + 1)
                for k in range(KD):
                    mm = pe.matmul(ps[0:w, 2, 36 * c:36 * c + 36], h2t[:, k, P * c:P * c + w], wrt[:, k, :],
                                   start=k == 0, stop=k == KD - 1, skip_group_check=True)
                mm.then_inc(logit_done, 1)

            for c in range(NC):
                if c >= 2:
                    pe.wait_ge(x2_ready, c - 1)
                project(c, range(NI, KD) if c < 2 else range(KD))
                if c >= 2:
                    turn_h2(c - 2)
                if c >= 3:
                    logits(c - 3)
            turn_h2(3)
            logits(2)
            turn_h2(4)
            logits(3)
            logits(4)
            pe.wait_ge(picks_ready, 1)
            for c in range(NC):
                for a in range(c + 1):
                    pe.matmul(ps[:, 3, NE * c:NE * c + NE], (tril if a == c else onesb)[:, :],
                              mb[:, NE * a:NE * a + NE], start=a == 0, stop=a == c, skip_group_check=True)
            for c in range(NC):
                mm = pe.matmul(ps[:, 3, NE * NC:NE * NC + NE], onesb[:, :], mb[:, NE * c:NE * c + NE],
                               start=c == 0, stop=c == NC - 1, skip_group_check=True)
            mm.then_inc(pos_done, 1)

            pe.wait_ge(places_ready, 1)
            pe.wait_ge(entries_ready, 2 * 3)
            pe.wait_ge(x2_ready, NC)
            for half in range(2):
                for k in range(2):
                    for c in range(NC):
                        mm = pe.matmul(ps[TILE * half:TILE * half + TILE, 4, 0:3 * PAIRS], place[k][:, c, :],
                                       entry[k][:, c, :, :].rearrange("p (g h) f -> p h g f", h=2)[:, half],
                                       start=k == 0 and c == 0, stop=k == 1 and c == NC - 1, skip_group_check=True)
            mm.then_inc(tab_summed, 1)

            def turn(g, s, n):
                pe.wait_ge(gathered[s], n * 16 + 16)
                if not peeled(g) or g >= 1:
                    pe.wait_ge(xt_ready, g)
                for k in range(KD):
                    mm = pe.transpose(ps[:, k // 4, P * (k % 4):P * (k % 4) + P], xg[s][:, P * k:P * k + P], ident[:, :])
                mm.then_inc(xg_turned, 1)

            def gate_up(g, s, n, half):
                q = 2 * s + half
                pe.wait_ge(wi_loaded[q], n * 16 + 16)
                if half == 0:
                    pe.wait_ge(xt_ready, g + 1)
                if peeled(g) and g == 0 and half == 1:
                    pe.wait_ge(ent_ready, 1)
                if not peeled(g) or g >= 1:
                    pe.wait_ge(act_ready, g * 2 + half - 1)
                for m in range(4):
                    for k in range(KD):
                        mm = pe.matmul(ps[:, 2 + half, TILE * m:TILE * m + TILE], wi[q][:, k, P * m:P * m + P],
                                       xt[s][:, k, TILE * half:TILE * half + TILE],
                                       start=k == 0, stop=k == KD - 1, skip_group_check=True)
                mm.then_inc(gu_done, 1)

            def down(g, s, n):
                for half in range(2):
                    pe.wait_ge(wo_loaded[2 * s + half], n * 16 + 16)
                pe.wait_ge(act_ready, g * 2 + 2)
                if not peeled(g) or g >= 1:
                    pe.wait_ge(yg_ready, g)
                for m in range(2):
                    for k in range(2):
                        for half in range(2):
                            mm = pe.matmul(ps[TILE * half:TILE * half + TILE, 4 + m, :], act2[half][:, k, :],
                                           wo[2 * s + half][:, k, 512 * m:512 * m + 512], start=k == 0, stop=k == 1,
                                           skip_group_check=True)
                mm.then_inc(y_done, 1)

            def step(g, s, n):
                if not (peeled(g) and g == PAIRS - 1):
                    turn(g + 1, (s + 1) % RING, n if s + 1 < RING else n + 1)
                gate_up(g, s, n, 0)
                if not (peeled(g) and g == 0):
                    down(g - 1, (s - 1) % RING, n if s > 0 else n - 1)
                gate_up(g, s, n, 1)

            for _ in range(WARM):
                pe.matmul(ps[:, 7, 0:P], ident[:, :], ident[:, :], start=True, stop=True)
            pe.wait_ge(tab_ready, 2)
            turn(0, 0, 0)
            pair_loop(pe, step, tail=1)
            down(PAIRS - 1, (PAIRS - 1) % RING, (PAIRS - 1) // RING)

            def more(n, e, t):
                pe.wait_ge(more_gathered, n * 16 + 16)
                pe.sem_inc(pe_passed, 1)
                for k in range(KD):
                    mm = pe.transpose(ps[:, k // 4, P * (k % 4):P * (k % 4) + TILE], xg[0][0:TILE, P * k:P * k + P],
                                      ident[0:TILE, 0:TILE])
                mm.then_inc(more_turned, 1)
                pe.wait_ge(more_xt, n + 1)
                pe.sem_inc(pe_passed, 1)
                for m in range(4):
                    for k in range(KD):
                        mm = pe.matmul(ps[:, 2, TILE * m:TILE * m + TILE], wi[0][:, k, P * m:P * m + P],
                                       xt[0][:, k, 0:TILE], start=k == 0, stop=k == KD - 1, skip_group_check=True)
                mm.then_inc(more_gu, 1)
                pe.wait_ge(more_act, n + 1)
                pe.sem_inc(pe_passed, 1)
                for m in range(2):
                    for k in range(2):
                        mm = pe.matmul(ps[0:TILE, 4 + m, :], act2[0][:, k, :], wo[0][:, k, 512 * m:512 * m + 512],
                                       start=k == 0, stop=k == 1)
                mm.then_inc(more_rows, 1)

            each_further_tile(pe, more)

        @block.scalar
        def _(act):
            def square_sum(out, src, acc):
                return act.activation(out, src, ACT.Square, accum_out=acc)

            def sumsq_input(c):
                w = ROWS[c]
                act.wait_ge(x_loaded[c], 32 if c in (0, 4) else 16)
                if c >= 1:
                    act.wait_ge(ssq_ready, c)
                square_sum(sq1[0:w, :], x[0:w, c, :], stat[0:w, c:c + 1]).then_inc(ssq_ready, 1)

            def copy_v(c):
                w = ROWS[c]
                act.wait_ge(v_done, c + 1)
                act.copy(v[0:w, c, :], ps[0:w, 4 + c % 2, :]).then_inc(v_ready, 1)

            act.wait_ge(small_turned, 1)
            act.copy(vt[:, :], ps[:, 7, 0:24]).then_inc(small_ready, 1)
            for c in range(NC):
                sumsq_input(c)
            for c in range(3):
                copy_v(c)
            act.wait_ge(small_turned, 2)
            act.copy(cwt[:, :, :], ps[:, 7, 0:NI * TAPS].rearrange("p (i j) -> p i j", i=NI)).then_inc(small_ready, 1)
            act.wait_ge(small_turned, 3)
            act.copy(u[:, :, US:US + HIST], ps[:, 6, 0:NI * HIST].rearrange("p (i j) -> p i j", i=NI)).then_inc(small_ready, 1)
            def upper(j):
                act.wait_ge(win_loaded[j % WSLOTS], 16 * (j // WSLOTS + 1))
                if j >= HSLOTS:
                    act.wait_ge(proj_done, j - HSLOTS + 1)
                act.copy(w_hi[j % HSLOTS], win[j % WSLOTS]).then_inc(w_hi_ready, 1)

            for j in range(HSLOTS):
                upper(j)
            for c in range(3, NC):
                copy_v(c)
            for i in range(NI):
                act.wait_ge(proj_done, 2 * i + 1)
                if i >= 1:
                    act.wait_ge(u_done, i)
                act.activation(sgm.rearrange("p (a t) -> p a t", a=2), ps[:, 0:2, 0:HALF], ACT.Sigmoid).then_inc(sig_done, 1)
                upper(2 * i + HSLOTS)
                upper(2 * i + HSLOTS + 1)
            for i in range(NI):
                act.wait_ge(proj_done, 9 + 2 * i)
                act.activation(kt[:, i, :].rearrange("p (a t) -> p a t", a=2), ps[:, 0:2, 0:HALF], ACT.Copy).then_inc(qk_done, 1)
                if 8 + 2 * i + HSLOTS < 16:
                    upper(8 + 2 * i + HSLOTS)
                act.wait_ge(proj_done, 10 + 2 * i)
                act.activation(qt[:, i, :].rearrange("p (a t) -> p a t", a=2), ps[:, 2:4, 0:HALF], ACT.Copy,
                               scale=HD ** -0.5).then_inc(qk_done, 1)
                if 9 + 2 * i + HSLOTS < 16:
                    upper(9 + 2 * i + HSLOTS)
            for b in range(8):
                act.wait_ge(ck_turned, b + 1)
                act.copy(ckt[:, :, P * b:P * b + P], ps[:, 6 + b % 2, :].rearrange("p (i t) -> p i t", i=NI)).then_inc(ckt_ready, 1)
            act.preload_act_table_set("natural_log_exp_and_others")

            def weights(s):
                st = steps[s]
                (r0, r1), n = st["rows"], st["n"]
                act.wait_ge(zr_ready, s + 1)
                if s >= 3:
                    act.wait_ge(av_done, s - 2)
                act.activation(wt[s % 3][r0:r1, 0:n], ps[r0:r1, s % 4, 0:n], ACT.Exp).then_inc(w_ready, 1)

            for s in range(NS + 2):
                if s < NS:
                    st = steps[s]
                    (r0, r1), n = st["rows"], st["n"]
                    a = za[s % 3][r0:r1, 0:n]
                    act.wait_ge(zc_ready, s + 1)
                    act.activation(a, a, ACT.Exp).then_inc(e_done, 1)
                i = s - LN_STEP - 2
                if 0 <= i < NI:
                    act.wait_ge(dev_ready, i + 1)
                    act.square(lnsq[:, i, :], yc[:, i, :]).then_inc(devsq_ready, 1)
                if s == LN_STEP + 11:
                    act.wait_ge(lnv_ready, 1)
                    act.activation(lnr, lnv, ACT.Ln).then_inc(lnl_done, 1)
                    act.wait_ge(lnl_done, 1)
                    act.activation(lnr, lnr, ACT.Exp, scale=-0.5).then_inc(lnr_done, 1)
                if s >= 2:
                    weights(s - 2)
                if s < NS:
                    act.wait_ge(e_done, s + 1)
                    act.activation(a, a, ACT.Ln, bias=1.0).then_inc(l_done, 1)

            for i in range(NI):
                act.wait_ge(norm_ready, i + 1)
                act.activation(mixt[:, i, :], yc[:, i, :], ACT.Silu, bias=vt[:, 16 + i:17 + i],
                               scale=vt[:, 12 + i:13 + i]).then_inc(mixa_ready, 1)
            for c in range(NC):
                w = ROWS[c]
                act.wait_ge(ko_turned, c + 1)
                if c >= 2:
                    act.wait_ge(ko_stored[c % 2], 16 * (c // 2))
                act.copy(ko[c % 2][0:w, :], ps[0:w, 6 + c % 2, :]).then_inc(ko_ready, 1)
            for b in range(2):
                act.wait_ge(co_turned, b + 1)
                act.copy(co[b][0:HIST, :], ps[0:HIST, b, :]).then_inc(co_ready, 1)

            def copy_h2t(c):
                w = ROWS[c]
                act.wait_ge(h2_turned, c + 1)
                act.copy(h2t[:, :, P * c:P * c + w],
                         ps[:, 0:2, :].rearrange("p b (k t) -> p (b k) t", t=P)[:, :, 0:w]).then_inc(h2t_ready, 1)

            for c in range(NC):
                w = ROWS[c]
                act.wait_ge(x2_ready, c + 1)
                if c >= 1:
                    act.wait_ge(ssq2_ready, c)
                square_sum(sq2[0:w, :], x[0:w, c, :], stat[0:w, 8 + c:9 + c]).then_inc(ssq2_ready, 1)
                if c >= 2:
                    copy_h2t(c - 2)
            copy_h2t(3)
            copy_h2t(4)
            act.wait_ge(gsub_ready, 1)
            act.activation(gex, gex, ACT.Exp).then_inc(gexp_ready, 1)
            act.wait_ge(esub_ready, 1)
            act.activation(ex, ex, ACT.Exp).then_inc(eexp_ready, 1)

            def silu(g, half):
                act.wait_ge(gu_done, g * 2 + half + 1)
                if not peeled(g) or g >= 1:
                    act.wait_ge(act_ready, g * 2 + half - 1)
                act.activation(sil[half], ps[:, 2 + half, 0:2 * TILE].rearrange("p (k t) -> p k t", k=2),
                               ACT.Silu).then_inc(sil_ready, 1)

            def gated_rows(g, s, n):
                act.wait_ge(y_done, g + 1)
                act.wait_ge(gat_ready, g + 1)
                if not peeled(g) or g >= RING:
                    act.wait_ge(scattered[s], n * 16)
                act.activation(yg[s].rearrange("p (m n) -> p m n", m=2), ps[:, 4:6, :],
                               ACT.Copy, scale=gat[s]).then_inc(yg_ready, 1)

            def step(g, s, n):
                silu(g, 0)
                if not (peeled(g) and g == 0):
                    gated_rows(g - 1, (s - 1) % RING, n if s > 0 else n - 1)
                silu(g, 1)

            pair_loop(act, step, tail=1)
            gated_rows(PAIRS - 1, (PAIRS - 1) % RING, (PAIRS - 1) // RING)

            def more(n, e, t):
                act.wait_ge(more_gu, n + 1)
                act.activation(sil[0], ps[:, 2, 0:2 * TILE].rearrange("p (k t) -> p k t", k=2), ACT.Silu).then_inc(more_sil, 1)
                act.wait_ge(more_rows, n + 1)
                act.activation(yg[0][0:TILE].rearrange("p (m n) -> p m n", m=2), ps[0:TILE, 4:6, :], ACT.Copy,
                               scale=more_tab[:, 2:3]).then_inc(more_scaled, 1)

            each_further_tile(act, more)

            for c in range(NC):
                w = ROWS[c]
                act.wait_ge(sum_ready, c + 1)
                if c >= 1:
                    act.wait_ge(ssq3_ready, c)
                square_sum(sq3[0:w, :], x[0:w, c, :], stat[0:w, 16 + c:17 + c]).then_inc(ssq3_ready, 1)
                if c - 1 in POOL_NORMS:
                    act.wait_ge(rstd_ready, ROOTS_BEFORE + c)
                    act.activation(yo[c - 1], x[:, c - 1, :], ACT.Copy, scale=stat[:, 39 + c:40 + c]).then_inc(scaled, 1)

        @block.vector
        def _(dve):
            chain = [0]
            rooted = [0]

            def halves(t):
                return t.rearrange("p (a t) -> p a t", a=2)

            def link(ins):
                chain[0] += 1
                ins.then_inc(dve_chain, 1)
                dve.wait_ge(dve_chain, chain[0])

            def rstd(dst, src, scale):
                dve.tensor_scalar(dst, src, scale, EPS, ALU.mult, ALU.add).then_inc(var_ready, 1)
                rooted[0] += 1
                dve.wait_ge(rstd_ready, rooted[0])

            def scale_input(c):
                w = ROWS[c]
                dve.wait_ge(ssq_ready, c + 1)
                rstd(stat[0:w, 24 + c:25 + c], stat[0:w, c:c + 1], 1.0 / D)
                if c >= 2:
                    dve.wait_ge(h_turned, c - 1)
                dve.tensor_scalar(h1[c % 2][0:w, :], x[0:w, c, :], stat[0:w, 24 + c:25 + c], None,
                                  ALU.mult).then_inc(h_ready, 1)

            def copy_ht(c):
                w = ROWS[c]
                dve.wait_ge(h_turned, c + 1)
                pt = ps[:, 2 * (c % 2):2 * (c % 2) + 2, :].rearrange("p b (k t) -> p (b k) t", t=P)
                dve.tensor_tensor(ht[:, :, P * c:P * c + w], pt[:, :, 0:w],
                                  vt[:, 0:KD].unsqueeze(2).broadcast_to([P, KD, w]), ALU.mult).then_inc(ht_ready, 1)

            scale_input(0)
            scale_input(1)
            dve.wait_ge(small_ready, 1)
            for c in range(NC):
                copy_ht(c)
                if c + 2 < NC:
                    scale_input(c + 2)

            for c in range(NC):
                cols = slice(P * c, P * c + ROWS[c])
                dve.wait_ge(ht_ready, c + 1)
                dve.tensor_copy(ht_hi[:, :, cols], ht[:, :, cols]).then_inc(ht_hi_ready, 1)
            for c in range(NC):
                cols = slice(P * c, P * c + ROWS[c])
                dve.wait_ge(ht_hi_ready, c + 1)
                dve.wait_ge(v_done, c + 1)
                dve.tensor_tensor(ht_lo[:, :, cols], ht[:, :, cols], ht_hi[:, :, cols].bitcast(F32), ALU.subtract).then_inc(ht_lo_ready, 1)

            def tap(i, j):
                if j == 0:
                    link(dve.tensor_scalar(conv[:, i, :], u[:, i, 0:CW], cwt[:, i, 0:1], None, ALU.mult))
                else:
                    link(dve.scalar_tensor_tensor(conv[:, i, :], u[:, i, j:j + CW], cwt[:, i, j:j + 1],
                                                  conv[:, i, :], ALU.mult, ALU.add))
                if j == TAPS - 1:
                    for dst, src in ((yc[:, i, 0:TP], conv[:, i, 0:TP]), (yc[:, i, S0:COLS], conv[:, i, US:US + TS])):
                        dve.tensor_scalar(dst, src, vt[:, 8 + i:9 + i], None, ALU.add).then_inc(yc_ready, 1)

            CW = UW - HIST
            taps = [(i, j) for i in range(NI) for j in range(TAPS)]
            dve.wait_ge(small_ready, 3)
            for i in range(NI):
                dve.wait_ge(proj_done, 2 * i + 2)
                dve.wait_ge(sig_done, i + 1)
                dve.tensor_tensor(u[:, i, HIST:HIST + HALF], ps[:, 2, 0:HALF], sgm[:, 0:HALF], ALU.mult).then_inc(conv_done, 1)
                dve.tensor_tensor(u[:, i, HIST + HALF:HIST + TP], ps[:, 3, 0:TP - HALF], sgm[:, HALF:TP], ALU.mult).then_inc(conv_done, 1)
                dve.tensor_tensor(u[:, i, UW - TS:UW], ps[:, 3, S0 - HALF:HALF], sgm[:, S0:COLS], ALU.mult).then_inc(u_done, 1)
                dve.wait_ge(conv_done, 2 * i + 2)
                dve.wait_ge(u_done, i + 1)
                for _ in range(TAPS_EARLY[i]):
                    tap(*taps.pop(0))

            def deviation(i):
                if i == 0:
                    dve.wait_ge(mean_done, 1)
                    dve.wait_ge(yc_ready, 2 * NI)
                dve.scalar_tensor_tensor(halves(yc[:, i, :]), ps[:, 6:8, 0:HALF], 1.0 / CC,
                                         halves(yc[:, i, :]), ALU.mult, ALU.add).then_inc(dev_ready, 1)

            def variances():
                dve.wait_ge(var_done, 1)
                dve.tensor_scalar(halves(lnv), ps[:, 6:8, 0:HALF], -1.0 / CC, EPS, ALU.mult, ALU.add).then_inc(lnv_ready, 1)

            def refine(j):
                if j == 0:
                    dve.wait_ge(lnr_done, 1)
                    dve.wait_ge(lnv_ready, 1)
                    link(dve.tensor_tensor(lnt, lnr, lnr, ALU.mult))
                elif j == 1:
                    link(dve.tensor_tensor(lnt, lnt, lnv, ALU.mult))
                elif j == 2:
                    link(dve.tensor_scalar(lnt, lnt, -0.5, 1.5, ALU.mult, ALU.add))
                else:
                    link(dve.tensor_tensor(lnr, lnr, lnt, ALU.mult))
                    dve.wait_ge(dev_ready, NI)

            def normed(i):
                dve.tensor_tensor(yc[:, i, :], yc[:, i, :], lnr, ALU.mult).then_inc(norm_ready, 1)

            def clamp(s):
                st = steps[s]
                (r0, r1), n = st["rows"], st["n"]
                dve.wait_ge(z_ready, s + 1)
                if s >= 3:
                    dve.wait_ge(el_ready, s - 2)
                dve.tensor_scalar(za[s % 3][r0:r1, 0:n], ps[r0:r1, s % 4, 0:n], ZCLAMP, None, ALU.min).then_inc(zc_ready, 1)

            def softplus(s):
                st = steps[s]
                (r0, r1), n = st["rows"], st["n"]
                dve.wait_ge(l_done, s + 1)
                if s >= 3:
                    dve.wait_ge(zr_ready, s - 2)
                    dve.wait_ge(cs_ready, sums[s - 3])
                dve.tensor_tensor(el[s % 3][r0:r1, 0:n], ps[r0:r1, s % 4, 0:n], za[s % 3][r0:r1, 0:n],
                                  ALU.max).then_inc(el_ready, 1)

            def unit_out(s):
                st = steps[s]
                if not st["last"]:
                    return
                dve.wait_ge(av_done, s + 1)
                o = ps[:, unit_bank(st["unit"]), :]
                if "h" in st:
                    h = st["h"]
                    dve.tensor_copy(ot[:, 0:4, 64 * h:64 * h + 64],
                                    o[:, 0:256].rearrange("p (t d) -> p t d", t=4)).then_inc(o_ready, 1)
                else:
                    p0 = st["p0"]
                    dve.tensor_copy(ot[p0:p0 + 32, 4, :], o[p0:p0 + 32, :]).then_inc(o_ready, 1)

            for s in range(NS + 4):
                if s < NS:
                    clamp(s)
                if 0 <= s - LN_STEP - 1 < NI:
                    deviation(s - LN_STEP - 1)
                if s == LN_STEP + 10:
                    variances()
                if 0 <= s - LN_STEP - 12 < 4:
                    refine(s - LN_STEP - 12)
                if 0 <= s - LN_STEP - 16 < NI:
                    normed(s - LN_STEP - 16)
                if 1 <= s <= NS:
                    softplus(s - 1)
                for _ in range(TAPS_STEP):
                    if taps:
                        tap(*taps.pop(0))
                if s >= 4:
                    unit_out(s - 4)
            dve.wait_ge(o_ready, 2 + HEADS)
            q = 0
            for lo, w, cc in ((0, P, slice(0, 4)), (0, 64, slice(4, 5))):
                k = cc.stop - cc.start
                link(dve.tensor_tensor(osq[0:w, cc, :], ot[0:w, cc, :], ot[0:w, cc, :], ALU.mult))
                st8 = stat_o[0:w, q:q + k * HEADS]
                link(dve.tensor_reduce(st8, osq[0:w, cc, :].rearrange("p c (h d) -> p (c h) d", d=HD), AX.X, ALU.add))
                rstd(st8, st8, 1.0 / HD)
                o4 = ot[0:w, cc, :].rearrange("p c (h d) -> p (c h) d", d=HD)
                ins = dve.tensor_tensor(o4, o4, st8.unsqueeze(2).broadcast_to([w, k * HEADS, HD]), ALU.mult)
                q += k * HEADS
                if q < NC * HEADS:
                    link(ins)
                else:
                    ins.then_inc(onorm_ready, 1)
            for c in range(NC):
                w = ROWS[c]
                dve.wait_ge(o_turned, c + 1)
                dve.tensor_tensor(mixt[:, NI:2 * NI, P * c:P * c + w],
                                  ps[:, 2 + c % 2, :].rearrange("p (i t) -> p i t", i=NI)[:, :, 0:w],
                                  vt[:, 20:24].unsqueeze(2).broadcast_to([P, NI, w]), ALU.mult).then_inc(mixb_ready, 1)

            dve.wait_ge(router_loaded, 16 * 5)
            for c in range(NC):
                w = ROWS[c]
                dve.wait_ge(res_done, c + 1)
                dve.tensor_tensor(x[0:w, c, :].rearrange("p (a n) -> p a n", a=2), x[0:w, c, :].rearrange("p (a n) -> p a n", a=2),
                                  ps[0:w, 4 + 2 * (c % 2):6 + 2 * (c % 2), :], ALU.add).then_inc(x2_ready, 1)
                dve.wait_ge(ssq2_ready, c + 1)
                rstd(stat[0:w, 32 + c:33 + c], stat[0:w, 8 + c:9 + c], 1.0 / D)
                if c >= 2:
                    dve.wait_ge(h2_turned, c - 1)
                    dve.wait_ge(h2_stored[c % 2], 16 * (c // 2))
                dve.scalar_tensor_tensor(h2[c % 2][0:w, :], x[0:w, c, :], stat[0:w, 32 + c:33 + c], gff[0:w, :],
                                         ALU.mult, ALU.mult).then_inc(h2_ready, 1)

            def v5(k):
                return sm[:, 5 * k:5 * k + 5]

            def wide(t, n):
                return t.unsqueeze(2).broadcast_to([P, NC, n])

            def over(t, n):
                return t.unsqueeze(1).broadcast_to([P, NC, n])

            def c3(t):
                return t.rearrange("p (c n) -> p c n", c=NC)

            gmax, gsum, m1, m2, esum, e2, first, t0, t1, pg, p1, p2, at1, at2 = (v5(k) for k in range(14))
            beyond = v5(14)
            low2 = [sm[:, 104 + 10 * k:104 + 10 * k + 2 * NC].rearrange("p (c f) -> p c f", f=2) for k in range(2)]
            dve.wait_ge(router_loaded, 16 * 5)
            dve.wait_ge(zero_ready, 9)
            link(dve.memset(valid[0:64, 4:5], 1.0))
            link(dve.tensor_scalar(t0, colid, float(TP), None, ALU.is_lt))
            link(dve.tensor_scalar(t1, colid, float(S0), None, ALU.is_ge))
            link(dve.tensor_tensor(t0, t0, t1, ALU.add))
            link(dve.tensor_tensor(valid[:, :], valid[:, :], t0, ALU.mult))
            link(dve.tensor_scalar(beyond, valid[:, :], -BIGF, BIGF, ALU.mult, ALU.add))
            for k in range(2):
                link(dve.tensor_copy(ent[k][:, :, 0], colid))
                link(dve.tensor_scalar(ent[k][:, :, 1], colid, float(COLS * k), None, ALU.add))
                link(dve.tensor_scalar(low2[k], ent[k][:, :, 0:2], -BIGF, None, ALU.add))
            dve.wait_ge(logit_done, NC)
            for c in range(NC):
                w = ROWS[c]
                link(dve.tensor_tensor(lg[0:w, c, :], ps[0:w, 2, 36 * c:36 * c + 36], bias36[0:w, :], ALU.add))
            lgg = lg[:, :, 0:NG]
            lge = lg[:, :, NG:NG + NE]
            link(dve.tensor_reduce(gmax, lgg, AX.X, ALU.max))
            dve.tensor_tensor(c3(gex), lgg, wide(gmax, NG), ALU.subtract).then_inc(gsub_ready, 1)

            def first_of(dst, src, top, iota, n, scratch):
                link(dve.tensor_tensor(c3(scratch), src, wide(top, n), ALU.is_equal))
                link(dve.scalar_tensor_tensor(c3(scratch), c3(scratch), -1000.0, over(iota, n), ALU.mult, ALU.add))
                link(dve.tensor_reduce(first, c3(scratch), AX.X, ALU.min))
                link(dve.tensor_tensor(c3(dst), c3(scratch), wide(first, n), ALU.is_equal))

            first_of(og, lgg, gmax, io4, NG, tmp[:, 0:NC * NG])
            link(dve.tensor_scalar(og, og, -NEG, NEG, ALU.mult, ALU.add))
            link(dve.tensor_tensor(lm.rearrange("p (c g e) -> p c g e", c=NC, g=NG), lge.rearrange("p c (g e) -> p c g e", g=NG),
                                   c3(og).unsqueeze(3).broadcast_to([P, NC, NG, EPG]), ALU.add))
            link(dve.tensor_reduce(m1, c3(lm), AX.X, ALU.max))
            dve.tensor_tensor(c3(ex), c3(lm), wide(m1, NE), ALU.subtract).then_inc(esub_ready, 1)
            first_of(o1, c3(lm), m1, io32, NE, eqm)
            link(dve.scalar_tensor_tensor(eqm, o1, 2 * NEG, lm, ALU.mult, ALU.add))
            link(dve.tensor_reduce(m2, c3(eqm), AX.X, ALU.max))
            first_of(o2, c3(eqm), m2, io32, NE, tmp)
            link(dve.tensor_tensor(c3(o1), c3(o1), wide(valid[:, :], NE), ALU.mult))
            link(dve.tensor_tensor(c3(o2), c3(o2), wide(valid[:, :], NE), ALU.mult))
            dve.tensor_tensor(mb, o1, o2, ALU.add).then_inc(picks_ready, 1)
            dve.wait_ge(gexp_ready, 1)
            link(dve.tensor_reduce(gsum, c3(gex), AX.X, ALU.add))
            link(dve.reciprocal(pg, gsum))
            dve.wait_ge(eexp_ready, 1)
            link(dve.tensor_reduce(esum, c3(ex), AX.X, ALU.add))
            link(dve.tensor_tensor(tmp, ex, o2, ALU.mult))
            link(dve.tensor_reduce(e2, c3(tmp), AX.X, ALU.add))
            link(dve.reciprocal(p1, esum))
            link(dve.tensor_tensor(p2, e2, p1, ALU.mult))
            link(dve.tensor_tensor(t0, p1, p2, ALU.add))
            link(dve.reciprocal(t0, t0))
            link(dve.tensor_tensor(t0, t0, pg, ALU.mult))
            link(dve.tensor_tensor(ent[0][:, :, 2], p1, t0, ALU.mult))
            link(dve.tensor_tensor(ent[1][:, :, 2], p2, t0, ALU.mult))
            for k, o in enumerate((o1, o2)):
                for f in range(3):
                    val = low2[k][:, :, f] if f < 2 else ent[k][:, :, 2]
                    dve.tensor_tensor(entry[k][:, :, :, f], c3(o), val.unsqueeze(2).broadcast_to([P, NC, NE]),
                                      ALU.mult).then_inc(entries_ready, 1)
            dve.wait_ge(pos_done, 1)
            for k, (o, at) in enumerate(((o1, at1), (o2, at2))):
                link(dve.tensor_tensor(tmp, ps[:, 3, 0:NC * NE], o, ALU.mult))
                link(dve.tensor_reduce(at, c3(tmp), AX.X, ALU.add))
                ins = dve.tensor_tensor(place[k], iotile.unsqueeze(1).broadcast_to([P, NC, TILE]), wide(at, TILE), ALU.is_equal)
                if k == 0:
                    link(ins)
                else:
                    ins.then_inc(places_ready, 1)
            dve.wait_ge(tab_summed, 1)
            sums3 = ps[:, 4, 0:3 * PAIRS].rearrange("p (g f) -> p g f", f=3)
            dve.tensor_scalar(tab[:, :, 0:2], sums3[:, :, 0:2], BIGF, None, ALU.add).then_inc(tab_ready, 1)
            dve.tensor_copy(tab[:, :, 2:3], sums3[:, :, 2:3]).then_inc(tab_ready, 1)
            for k, (o, at) in enumerate(((o1, at1), (o2, at2))):
                link(dve.tensor_tensor(c3(tmp), c3(o), over(ecol, NE), ALU.mult))
                link(dve.tensor_reduce(t0, c3(tmp), AX.X, ALU.add))
                link(dve.scalar_tensor_tensor(t0, at, float(NE), t0, ALU.mult, ALU.add))
                link(dve.tensor_tensor(adr[k], t0, beyond, ALU.add))
            link(dve.tensor_reduce(sm[0:1, 100:101], ps[0:1, 3, NE * NC:NE * NC + NE], AX.X, ALU.max))
            link(dve.tensor_copy(cnt[:, 0:NE], ps[0:1, 3, NE * NC:NE * NC + NE]))
            dve.tensor_copy(cnt[:, NE:NE + 1], sm[0:1, 100:101]).then_inc(ent_ready, 1)

            def copy_xt(g, s):
                dve.wait_ge(xg_turned, g + 1)
                if not peeled(g) or g >= RING:
                    dve.wait_ge(gu_done, (g - RING) * 2 + 2)
                dve.tensor_copy(xt[s], ps[:, 0:2, :].rearrange("p b (k t) -> p (b k) t", t=P)).then_inc(xt_ready, 1)

            def gate_times_up(g, half):
                dve.wait_ge(sil_ready, g * 2 + half + 1)
                if not peeled(g) or g >= 1:
                    dve.wait_ge(y_done, g)
                dve.tensor_tensor(act2[half], sil[half], ps[:, 2 + half, 2 * TILE:4 * TILE].rearrange("p (k t) -> p k t", k=2),
                                  ALU.mult).then_inc(act_ready, 1)

            def step(g, s, n):
                if not (peeled(g) and g == PAIRS - 1):
                    copy_xt(g + 1, (s + 1) % RING)
                for half in range(2):
                    gate_times_up(g, half)

            copy_xt(0, 0)
            pair_loop(dve, step, tail=1)

            def more(n, e, t):
                dve.wait_ge(more_turned, n + 1)
                dve.tensor_copy(xt[0][:, :, 0:TILE], ps[:, 0:2, :].rearrange("p b (k t) -> p (b k) t", t=P)[:, :, 0:TILE]).then_inc(more_xt, 1)
                dve.wait_ge(more_sil, n + 1)
                dve.tensor_tensor(act2[0], sil[0], ps[:, 2, 2 * TILE:4 * TILE].rearrange("p (k t) -> p k t", k=2),
                                  ALU.mult).then_inc(more_act, 1)

            each_further_tile(dve, more)

            def add_experts(c):
                w = ROWS[c]
                if c in POOL_ADDS:
                    dve.wait_ge(y01_ready, POOL_ADDS.index(c) + 1)
                else:
                    dve.wait_ge(y_loaded[c], 32 if c < 4 else 64)
                    link(dve.tensor_tensor(y0[c][0:w, :], y0[c][0:w, :], y1[c][0:w, :], ALU.add))
                dve.tensor_tensor(x[0:w, c, :], x[0:w, c, :], y0[c][0:w, :], ALU.add).then_inc(sum_ready, 1)

            def mean_square(c):
                w = ROWS[c]
                dve.wait_ge(ssq3_ready, c + 1)
                dve.tensor_scalar(stat[0:w, 40 + c:41 + c], stat[0:w, 16 + c:17 + c], 1.0 / D, EPS, ALU.mult, ALU.add).then_inc(var_ready, 1)
                rooted[0] += 1

            def norm_out(c):
                w = ROWS[c]
                if c in POOL_NORMS:
                    return
                dve.wait_ge(rstd_ready, before + c + 1)
                dve.scalar_tensor_tensor(yo[c][0:w, :], x[0:w, c, :], stat[0:w, 40 + c:41 + c], gfn[0:w, :],
                                         ALU.mult, ALU.mult).then_inc(yo_ready, 1)

            dve.wait_ge(gfn_loaded, 16)
            before = rooted[0]
            add_experts(0)
            for c in range(NC):
                if c + 1 < NC:
                    add_experts(c + 1)
                mean_square(c)
                if c >= 1:
                    norm_out(c - 1)
            norm_out(NC - 1)


_INS = ['x_prompt', 'x_sample', 'cache_k', 'cache_v', 'cache_conv', 'meta_tokens', 'g_mix', 'w_in',
        'conv_w', 'conv_b', 'conv_ln_g', 'conv_ln_b', 'g_sb', 'w_out', 'g_ffn', 'w_router_group',
        'b_router_group', 'w_router_expert', 'b_router_expert', 'w_expert_in', 'w_expert_out', 'g_final']
_OUTS = [(1, SEQ, D), (1, TS, D), (1, 1, TP, HEADS, HD), (1, 1, TP, HEADS, HD), (1, 1, HIST, CC),
         (1, 1, TS, HEADS, HD), (1, 1, TS, HEADS, HD), (1, 1, HIST, CC)]


def kernel(**inputs):
    import numpy as _np
    import concourse.bacc as _bacc
    from concourse import mybir as _mybir
    from concourse.bass_utils import run_bass_kernel_spmd as _run

    nc = _bacc.Bacc("TRN2", target_bir_lowering=False, num_devices=1)
    arrays, args = {}, []
    for name in _INS:
        a = _np.ascontiguousarray(inputs[name])
        arrays[f"in_{name}"] = a
        args.append(nc.dram_tensor(f"in_{name}", a.shape, _mybir.dt.from_np(a.dtype), kind="ExternalInput").ap())
    for i, shape in enumerate(_OUTS):
        args.append(nc.dram_tensor(f"out_{i}", shape, _mybir.dt.float32, kind="ExternalOutput").ap())
    build(nc, *args)
    r = _run(nc, [arrays], core_ids=[0])
    return tuple(r.results[0][f"out_{i}"] for i in range(len(_OUTS)))
```
